# Optimizing a Trainium2 kernel written in Bass

```python
import math
import jax
import jax.numpy as jnp
from jax import lax
import numpy as np
import jax, jax.numpy as jnp

D_MODEL = 1024
BATCH = 1
SEQ = 512
DEPTH = 1

GRID_W = 64
CTX_LEN = 256
NORM_EPS = 1e-6
N_MOD = 6

NA_HEADS = 16
NA_HEAD_DIM = 64
NA_WIDTH = NA_HEADS * NA_HEAD_DIM
NA_KH = 8
NA_KW = 16
ROPE_BASE = 10000.0

SSD_WIDTH = 2 * D_MODEL
SSD_HEAD_DIM = 64
SSD_HEADS = SSD_WIDTH // SSD_HEAD_DIM
SSD_GROUPS = 4
SSD_STATE = 128
SSD_CONV = 5
SSD_CHUNK = 128
SSD_XBC = SSD_WIDTH + 2 * SSD_GROUPS * SSD_STATE

N_EXPERTS = 16
EXPERT_FF = 2048
EC_CAPACITY_FACTOR = 2

IN_COLS = 3 * NA_WIDTH + SSD_WIDTH + SSD_XBC + 2 * SSD_HEADS + 2 * D_MODEL


def _rmsnorm(x, g):
    xf = x.astype(jnp.float32)
    xf = xf * lax.rsqrt(jnp.mean(xf * xf, axis=-1, keepdims=True) + NORM_EPS)
    return (xf * g.astype(jnp.float32)).astype(x.dtype)

def _modulate(x, g, shift, scale):
    return _rmsnorm(x, g) * (1 + scale) + shift

def _ada(cvec, w_ada, b_ada):
    mod = jax.nn.silu(cvec) @ w_ada + b_ada
    return jnp.split(mod, N_MOD, axis=-1)

def _split_in(p):
    offs = np.cumsum([NA_WIDTH, NA_WIDTH, NA_WIDTH, SSD_WIDTH, SSD_XBC, 2 * SSD_HEADS])
    return jnp.split(p, [int(o) for o in offs], axis=-1)

def _heads(t):
    return t.reshape(t.shape[0], t.shape[1], NA_HEADS, NA_HEAD_DIM)

def _rotate(t, pos):
    half = t.shape[-1] // 2
    inv_freq = ROPE_BASE ** (-jnp.arange(half, dtype=jnp.float32) / half)
    ang = pos.astype(jnp.float32)[:, None] * inv_freq[None, :]
    cos = jnp.cos(ang)[:, None, :].astype(t.dtype)
    sin = jnp.sin(ang)[:, None, :].astype(t.dtype)
    t1, t2 = t[..., :half], t[..., half:]
    return jnp.concatenate([t1 * cos - t2 * sin, t1 * sin + t2 * cos], axis=-1)

def _rope_2d(t, rows, cols):
    da = t.shape[-1] // 2
    return jnp.concatenate([_rotate(t[..., :da], rows), _rotate(t[..., da:], cols)], axis=-1)

def _neighbourhood_attention(q, k, v, k_ctx, v_ctx, rpb):
    Bsz, L, H, Dh = q.shape
    rows = L // GRID_W
    kh = min(NA_KH, rows)
    n_loc = kh * GRID_W
    scale = Dh ** -0.5
    qg = q.reshape(Bsz, rows, GRID_W, H, Dh)
    kg = k.reshape(Bsz, rows, GRID_W, H, Dh)
    vg = v.reshape(Bsz, rows, GRID_W, H, Dh)
    col = jnp.arange(GRID_W)
    col_start = jnp.clip(col - NA_KW // 2, 0, GRID_W - NA_KW)
    col_ok = (col[None, :] >= col_start[:, None]) & (col[None, :] < col_start[:, None] + NA_KW)
    col_idx = jnp.clip(col[None, :] - col[:, None] + NA_KW - 1, 0, 2 * NA_KW - 2)
    rpb_col = rpb[:, :, col_idx]
    mask = jnp.tile(col_ok, (1, kh))

    def row_block(r):
        r0 = jnp.clip(r - kh // 2, 0, rows - kh)
        q_r = lax.dynamic_index_in_dim(qg, r, axis=1, keepdims=False)
        k_r = lax.dynamic_slice_in_dim(kg, r0, kh, axis=1).reshape(Bsz, n_loc, H, Dh)
        v_r = lax.dynamic_slice_in_dim(vg, r0, kh, axis=1).reshape(Bsz, n_loc, H, Dh)
        bias = jnp.take(rpb_col, r0 + jnp.arange(kh) - r + NA_KH - 1, axis=1)
        bias = jnp.transpose(bias, (0, 2, 1, 3)).reshape(H, GRID_W, n_loc).astype(jnp.float32)
        s_loc = jnp.einsum('bqhd,bkhd->bhqk', q_r, k_r).astype(jnp.float32) * scale + bias
        s_loc = jnp.where(mask, s_loc, -jnp.inf)
        s_ctx = jnp.einsum('bqhd,bkhd->bhqk', q_r, k_ctx).astype(jnp.float32) * scale
        p = jax.nn.softmax(jnp.concatenate([s_loc, s_ctx], axis=-1), axis=-1).astype(v.dtype)
        return (jnp.einsum('bhqk,bkhd->bqhd', p[..., :n_loc], v_r)
                + jnp.einsum('bhqk,bkhd->bqhd', p[..., n_loc:], v_ctx))

    out = lax.map(row_block, jnp.arange(rows))
    return jnp.moveaxis(out, 0, 1).reshape(Bsz, L, H * Dh)

def _context_attention(q, k, v):
    Bsz, T, H, Dh = q.shape
    s = jnp.einsum('bqhd,bkhd->bhqk', q, k).astype(jnp.float32) * Dh ** -0.5
    p = jax.nn.softmax(s, axis=-1).astype(v.dtype)
    return jnp.einsum('bhqk,bkhd->bqhd', p, v).reshape(Bsz, T, H * Dh)

def _dwconv(x, w, b):
    nch = x.shape[-1]
    out = lax.conv_general_dilated(x, w.astype(x.dtype)[:, None, :], window_strides=(1,),
                                   padding=[(SSD_CONV // 2, SSD_CONV // 2)],
                                   dimension_numbers=('NWC', 'WIO', 'NWC'),
                                   feature_group_count=nch)
    return out + b

def _ssd_prep(xbc, dt_raw, conv_w, conv_b, dtb_f, dtb_b):
    Bsz, L, _ = xbc.shape
    xbc = jax.nn.silu(_dwconv(xbc, conv_w, conv_b))
    xs, Bm, Cm = jnp.split(xbc, [SSD_WIDTH, SSD_WIDTH + SSD_GROUPS * SSD_STATE], axis=-1)
    xs = xs.reshape(Bsz, L, SSD_HEADS, SSD_HEAD_DIM)
    Bm = Bm.reshape(Bsz, L, SSD_GROUPS, SSD_STATE)
    Cm = Cm.reshape(Bsz, L, SSD_GROUPS, SSD_STATE)
    dt_f = jax.nn.softplus(dt_raw[..., :SSD_HEADS] + dtb_f)
    dt_b = jax.nn.softplus(dt_raw[..., SSD_HEADS:] + dtb_b)
    return xs, Bm, Cm, dt_f, dt_b

def _ssd_scan(xs, dt, A, Bm, Cm, h0, return_y):
    Bsz, L, H, P = xs.shape
    nc = L // SSD_CHUNK
    R = H // SSD_GROUPS
    x = (xs * dt[..., None]).reshape(Bsz, nc, SSD_CHUNK, SSD_GROUPS, R, P)
    a = (dt * A).astype(jnp.float32).reshape(Bsz, nc, SSD_CHUNK, SSD_GROUPS, R)
    a_cs = jnp.cumsum(jnp.moveaxis(a, 2, -1), axis=-1)
    Bc = Bm.reshape(Bsz, nc, SSD_CHUNK, SSD_GROUPS, SSD_STATE)
    decay_to_end = jnp.exp(a_cs[..., -1:] - a_cs).astype(xs.dtype)
    states = jnp.einsum('bclgn,bcgrl,bclgrp->bcgrpn', Bc, decay_to_end, x)
    chunk_decay = jnp.exp(a_cs[..., -1]).astype(xs.dtype)

    def step(h, inp):
        dec, st = inp
        return dec[..., None, None] * h + st, h

    h_last, h_prev = lax.scan(step, h0.reshape(Bsz, SSD_GROUPS, R, P, SSD_STATE),
                              (jnp.moveaxis(chunk_decay, 1, 0), jnp.moveaxis(states, 1, 0)))
    h_last = h_last.reshape(Bsz, H, P, SSD_STATE)
    if not return_y:
        return None, h_last
    Cc = Cm.reshape(Bsz, nc, SSD_CHUNK, SSD_GROUPS, SSD_STATE)
    lower = jnp.tril(jnp.ones((SSD_CHUNK, SSD_CHUNK), dtype=bool))
    seg = a_cs[..., :, None] - a_cs[..., None, :]
    Lm = jnp.exp(jnp.where(lower, seg, -jnp.inf)).astype(xs.dtype)
    cb = jnp.einsum('bclgn,bcsgn->bcgls', Cc, Bc)
    y_diag = jnp.einsum('bcgls,bcgrls,bcsgrp->bclgrp', cb, Lm, x)
    y_off = jnp.einsum('bclgn,bcgrpn,bcgrl->bclgrp', Cc, jnp.moveaxis(h_prev, 0, 1),
                       jnp.exp(a_cs).astype(xs.dtype))
    return (y_diag + y_off).reshape(Bsz, L, H, P), h_last

def _bidir_ssd(xs, Bm, Cm, dt_f, dt_b, A_f, A_b, d_skip, h0_f, h0_b, return_y):
    flip = lambda t: jnp.flip(t, axis=1)
    y_f, h_f = _ssd_scan(xs, dt_f, A_f, Bm, Cm, h0_f, return_y)
    y_b, h_b = _ssd_scan(flip(xs), flip(dt_b), A_b, flip(Bm), flip(Cm), h0_b, return_y)
    if not return_y:
        return None, h_f, h_b
    return y_f + flip(y_b) + d_skip[:, None] * xs, h_f, h_b

def _ssd_gated_norm(y, z, g):
    Bsz, L = y.shape[:2]
    u = (y.reshape(Bsz, L, SSD_WIDTH) * jax.nn.silu(z)).astype(jnp.float32)
    u = u.reshape(Bsz, L, SSD_GROUPS, SSD_WIDTH // SSD_GROUPS)
    u = u * lax.rsqrt(jnp.mean(u * u, axis=-1, keepdims=True) + NORM_EPS)
    return (u.reshape(Bsz, L, SSD_WIDTH) * g.astype(jnp.float32)).astype(y.dtype)

def _merge(o_na, y_ssd, gates, w_br_na, w_br_ssd, w_out):
    g_na, g_ssd = jnp.split(gates, 2, axis=-1)
    u = jax.nn.sigmoid(g_na) * (o_na @ w_br_na) + jax.nn.sigmoid(g_ssd) * (y_ssd @ w_br_ssd)
    return u @ w_out

def _token_mixer(h, hc, w_in, na_rpb, conv_w, conv_b, a_log_f, a_log_b, dtb_f, dtb_b, d_skip,
                 ssd_norm, w_br_na, w_br_ssd, w_out, update_ctx):
    Bsz, L, _ = h.shape
    q, k, v, z, xbc, dt_raw, gates = _split_in(h @ w_in)
    qc, kc, vc, zc, xbcc, dtc, gates_c = _split_in(hc @ w_in)
    pos = jnp.arange(L)
    rows, cols = pos // GRID_W, pos % GRID_W
    o_na = _neighbourhood_attention(_rope_2d(_heads(q), rows, cols), _rope_2d(_heads(k), rows, cols),
                                    _heads(v), _heads(kc), _heads(vc), na_rpb)
    A_f, A_b = -jnp.exp(a_log_f), -jnp.exp(a_log_b)
    h0 = jnp.zeros((Bsz, SSD_HEADS, SSD_HEAD_DIM, SSD_STATE), h.dtype)
    y_c, hf_c, hb_c = _bidir_ssd(*_ssd_prep(xbcc, dtc, conv_w, conv_b, dtb_f, dtb_b),
                                 A_f, A_b, d_skip, h0, h0, update_ctx)
    y, _, _ = _bidir_ssd(*_ssd_prep(xbc, dt_raw, conv_w, conv_b, dtb_f, dtb_b),
                         A_f, A_b, d_skip, hf_c, hb_c, True)
    mix = _merge(o_na, _ssd_gated_norm(y, z, ssd_norm), gates, w_br_na, w_br_ssd, w_out)
    if not update_ctx:
        return mix, None
    o_na_c = _context_attention(_heads(qc), _heads(kc), _heads(vc))
    mix_c = _merge(o_na_c, _ssd_gated_norm(y_c, zc, ssd_norm), gates_c, w_br_na, w_br_ssd, w_out)
    return mix, mix_c

def _ec_moe(h, w_router, w_eg, w_eu, w_ed):
    Bsz, T, _ = h.shape
    cap = EC_CAPACITY_FACTOR * T // N_EXPERTS
    aff = jax.nn.softmax((h @ w_router).astype(jnp.float32), axis=-1)
    gate, idx = lax.top_k(jnp.transpose(aff, (0, 2, 1)), cap)
    b_idx = jnp.arange(Bsz)[:, None, None]
    xg = h[b_idx, idx]
    hid = jax.nn.silu(jnp.einsum('becd,edf->becf', xg, w_eg)) * jnp.einsum('becd,edf->becf', xg, w_eu)
    yo = jnp.einsum('becf,efd->becd', hid, w_ed) * gate[..., None].astype(h.dtype)
    return jnp.zeros_like(h).at[b_idx, idx].add(yo)

def _layer(x, ctx, c, c_ctx, w_ada, b_ada, n_pre_mix, n_post_mix, n_pre_ffn, n_post_ffn, w_in, na_rpb,
           conv_w, conv_b, a_log_f, a_log_b, dtb_f, dtb_b, d_skip, ssd_norm, w_br_na, w_br_ssd, w_out,
           w_router, w_eg, w_eu, w_ed, update_ctx):
    sh1, sc1, ga1, sh2, sc2, ga2 = _ada(c[:, None, :], w_ada, b_ada)
    csh1, csc1, cga1, csh2, csc2, cga2 = _ada(c_ctx, w_ada, b_ada)
    mix, mix_c = _token_mixer(_modulate(x, n_pre_mix, sh1, sc1), _modulate(ctx, n_pre_mix, csh1, csc1),
                              w_in, na_rpb, conv_w, conv_b, a_log_f, a_log_b, dtb_f, dtb_b, d_skip,
                              ssd_norm, w_br_na, w_br_ssd, w_out, update_ctx)
    x = x + ga1 * _rmsnorm(mix, n_post_mix)
    x = x + ga2 * _rmsnorm(_ec_moe(_modulate(x, n_pre_ffn, sh2, sc2), w_router, w_eg, w_eu, w_ed), n_post_ffn)
    if update_ctx:
        ctx = ctx + cga1 * _rmsnorm(mix_c, n_post_mix)
        ctx = ctx + cga2 * _rmsnorm(_ec_moe(_modulate(ctx, n_pre_ffn, csh2, csc2), w_router, w_eg, w_eu, w_ed),
                                    n_post_ffn)
    return x, ctx

def first_inputs(seed: int = 0) -> dict:
    key = jax.random.key(seed)
    ks = jax.random.split(key, 26)
    f32 = jnp.float32

    def nrm(k, shape, s):
        return jax.random.normal(k, shape, f32) * s

    dt0 = jnp.exp(jax.random.uniform(ks[14], (DEPTH, 2, SSD_HEADS), f32, math.log(1e-3), math.log(1e-1)))
    dt_bias = dt0 + jnp.log(-jnp.expm1(-dt0))
    a_log = jnp.log(jax.random.uniform(ks[15], (DEPTH, 2, SSD_HEADS), f32, 1.0, 16.0))
    return {
        'x': nrm(ks[0], (BATCH, SEQ, D_MODEL), 1.0),
        'c': nrm(ks[1], (BATCH, D_MODEL), 1.0),
        'ctx': nrm(ks[2], (BATCH, CTX_LEN, D_MODEL), 1.0),
        'c_ctx': nrm(ks[3], (D_MODEL,), 1.0),
        'w_ada': nrm(ks[4], (DEPTH, D_MODEL, N_MOD * D_MODEL), 0.5 * D_MODEL ** -0.5),
        'b_ada': nrm(ks[5], (DEPTH, N_MOD * D_MODEL), 0.02),
        'norm_pre_mix': 1.0 + nrm(ks[6], (DEPTH, D_MODEL), 0.02),
        'norm_post_mix': 1.0 + nrm(ks[7], (DEPTH, D_MODEL), 0.02),
        'norm_pre_ffn': 1.0 + nrm(ks[8], (DEPTH, D_MODEL), 0.02),
        'norm_post_ffn': 1.0 + nrm(ks[9], (DEPTH, D_MODEL), 0.02),
        'w_in': nrm(ks[10], (DEPTH, D_MODEL, IN_COLS), D_MODEL ** -0.5),
        'na_rpb': nrm(ks[11], (DEPTH, NA_HEADS, 2 * NA_KH - 1, 2 * NA_KW - 1), 0.1),
        'ssd_conv_w': nrm(ks[12], (DEPTH, SSD_CONV, SSD_XBC), SSD_CONV ** -0.5),
        'ssd_conv_b': nrm(ks[13], (DEPTH, SSD_XBC), 0.02),
        'ssd_a_log_fwd': a_log[:, 0],
        'ssd_a_log_bwd': a_log[:, 1],
        'ssd_dt_bias_fwd': dt_bias[:, 0],
        'ssd_dt_bias_bwd': dt_bias[:, 1],
        'ssd_d_skip': 1.0 + nrm(ks[16], (DEPTH, SSD_HEADS), 0.02),
        'ssd_norm': 1.0 + nrm(ks[17], (DEPTH, SSD_WIDTH), 0.02),
        'w_branch_na': nrm(ks[18], (DEPTH, NA_WIDTH, D_MODEL), NA_WIDTH ** -0.5),
        'w_branch_ssd': nrm(ks[19], (DEPTH, SSD_WIDTH, D_MODEL), SSD_WIDTH ** -0.5),
        'w_out': nrm(ks[20], (DEPTH, D_MODEL, D_MODEL), D_MODEL ** -0.5),
        'w_router': nrm(ks[21], (DEPTH, D_MODEL, N_EXPERTS), D_MODEL ** -0.5),
        'w_exp_gate': nrm(ks[22], (DEPTH, N_EXPERTS, D_MODEL, EXPERT_FF), D_MODEL ** -0.5),
        'w_exp_up': nrm(ks[23], (DEPTH, N_EXPERTS, D_MODEL, EXPERT_FF), D_MODEL ** -0.5),
        'w_exp_down': nrm(ks[24], (DEPTH, N_EXPERTS, EXPERT_FF, D_MODEL), EXPERT_FF ** -0.5),
    }

def first_block(x, c, ctx, c_ctx, w_ada, b_ada, norm_pre_mix, norm_post_mix, norm_pre_ffn, norm_post_ffn,
              w_in, na_rpb, ssd_conv_w, ssd_conv_b, ssd_a_log_fwd, ssd_a_log_bwd, ssd_dt_bias_fwd,
              ssd_dt_bias_bwd, ssd_d_skip, ssd_norm, w_branch_na, w_branch_ssd, w_out, w_router,
              w_exp_gate, w_exp_up, w_exp_down):
    for i in range(DEPTH):
        x, ctx = _layer(x, ctx, c, c_ctx, w_ada[i], b_ada[i], norm_pre_mix[i], norm_post_mix[i],
                        norm_pre_ffn[i], norm_post_ffn[i], w_in[i], na_rpb[i], ssd_conv_w[i], ssd_conv_b[i],
                        ssd_a_log_fwd[i], ssd_a_log_bwd[i], ssd_dt_bias_fwd[i], ssd_dt_bias_bwd[i],
                        ssd_d_skip[i], ssd_norm[i], w_branch_na[i], w_branch_ssd[i], w_out[i], w_router[i],
                        w_exp_gate[i], w_exp_up[i], w_exp_down[i], i < DEPTH - 1)
    return x


RW_HEADS = 8
RW_HEAD_DIM = 64
RW_DIM = RW_HEADS * RW_HEAD_DIM
W_LORA = 64
A_LORA = 64
G_LORA = 128
GN_EPS = 64e-5
MLA_HEADS = 8
QK_NOPE = 64
QK_ROPE = 32
V_HEAD = 64
Q_LORA = 384
KV_LORA = 256
ROPE_THETA = 10000.0
Q_BLOCK = 128
N_GROUPS = 4
EXPERTS_PER_GROUP = 8
N_EXPERTS_2 = N_GROUPS * EXPERTS_PER_GROUP
TOP_K = 2
D_EXPERT = 256
EXPERT_BLOCK = 256

RW_COLS = 3 * RW_DIM + W_LORA + A_LORA + G_LORA
MLA_COLS = Q_LORA + KV_LORA + QK_ROPE
GATE_COLS = 2 * D_MODEL
IN_COLS_2 = RW_COLS + MLA_COLS + GATE_COLS


def rmsnorm(x, g):
    xf = x.astype(jnp.float32)
    y = xf * lax.rsqrt(jnp.mean(xf * xf, axis=-1, keepdims=True) + NORM_EPS)
    return (y * g.astype(jnp.float32)).astype(x.dtype)

def rope(t, cos, sin):
    t1, t2 = jnp.split(t, 2, axis=-1)
    return jnp.concatenate([t1 * cos - t2 * sin, t2 * cos + t1 * sin], axis=-1)

def rwkv7_mix(z_in, mu, w0, w_up, a0, a_up, g_up, k_k, k_a, r_k, gn_w, gn_b):
    B, S, _ = z_in.shape
    dt = z_in.dtype
    prev = jnp.pad(z_in, ((0, 0), (1, 0), (0, 0)))[:, :-1]
    z = z_in + (prev - z_in) * mu
    r, k, v, wd, ad, gd = jnp.split(
        z, [RW_DIM, 2 * RW_DIM, 3 * RW_DIM, 3 * RW_DIM + W_LORA, 3 * RW_DIM + W_LORA + A_LORA], axis=-1)
    w_log = -jax.nn.softplus(-(w0 + jnp.tanh(wd) @ w_up).astype(jnp.float32)) - 0.5
    decay = jnp.exp(-jnp.exp(w_log))
    a = jax.nn.sigmoid(a0 + ad @ a_up)
    g = jax.nn.sigmoid(gd) @ g_up

    def heads(t):
        return t.reshape(B, S, RW_HEADS, RW_HEAD_DIM).astype(jnp.float32)

    kk = heads(k * k_k)
    kk = kk / jnp.maximum(jnp.sqrt(jnp.sum(kk * kk, axis=-1, keepdims=True)), 1e-12)
    k = k * (1.0 + (a - 1.0) * k_a)
    r_h, k_h, v_h, a_h, w_h = heads(r), heads(k), heads(v), heads(a), heads(decay)

    def step(state, inp):
        r_t, w_t, k_t, v_t, kk_t, a_t = inp
        sa = jnp.einsum('bhvk,bhk->bhv', state, -kk_t)
        state = (state * w_t[:, :, None, :]
                 + sa[..., None] * (kk_t * a_t)[:, :, None, :]
                 + v_t[..., None] * k_t[:, :, None, :])
        return state, jnp.einsum('bhvk,bhk->bhv', state, r_t)

    xs = tuple(jnp.moveaxis(t, 1, 0) for t in (r_h, w_h, k_h, v_h, kk, a_h))
    s0 = jnp.zeros((B, RW_HEADS, RW_HEAD_DIM, RW_HEAD_DIM), jnp.float32)
    _, ys = lax.scan(step, s0, xs)
    y = jnp.moveaxis(ys, 0, 1)
    mean = jnp.mean(y, axis=-1, keepdims=True)
    var = jnp.mean(jnp.square(y - mean), axis=-1, keepdims=True)
    y = ((y - mean) * lax.rsqrt(var + GN_EPS)).reshape(B, S, RW_DIM)
    y = y * gn_w.astype(jnp.float32) + gn_b.astype(jnp.float32)
    bonus = jnp.sum(r_h * k_h * r_k.astype(jnp.float32), axis=-1, keepdims=True) * v_h
    y = y + bonus.reshape(B, S, RW_DIM)
    return (y * g.astype(jnp.float32)).astype(dt)

def mla_mix(q_d, kv_d, kr_raw, cos, sin, g_qa, w_q_up, g_kva, w_kv_up):
    B, S, _ = q_d.shape
    q = (rmsnorm(q_d, g_qa) @ w_q_up).reshape(B, S, MLA_HEADS, QK_NOPE + QK_ROPE)
    q_nope, q_rope = q[..., :QK_NOPE], q[..., QK_NOPE:]
    kv = (rmsnorm(kv_d, g_kva) @ w_kv_up).reshape(B, S, MLA_HEADS, QK_NOPE + V_HEAD)
    k_nope, v = kv[..., :QK_NOPE], kv[..., QK_NOPE:]
    q_rope = rope(q_rope, cos[:, :, None, :], sin[:, :, None, :])
    k_rope = rope(kr_raw, cos, sin)
    scale = 1.0 / math.sqrt(QK_NOPE + QK_ROPE)
    outs = []
    for start in range(0, S, Q_BLOCK):
        end = min(start + Q_BLOCK, S)
        s = (jnp.einsum('bqhd,bkhd->bhqk', q_nope[:, start:end], k_nope[:, :end])
             + jnp.einsum('bqhr,bkr->bhqk', q_rope[:, start:end], k_rope[:, :end]))
        s = s.astype(jnp.float32) * scale
        causal = jnp.arange(end)[None, :] <= jnp.arange(start, end)[:, None]
        p = jax.nn.softmax(jnp.where(causal, s, -jnp.inf), axis=-1).astype(v.dtype)
        outs.append(jnp.einsum('bhqk,bkhd->bqhd', p, v[:, :end]))
    return jnp.concatenate(outs, axis=1).reshape(B, S, MLA_HEADS * V_HEAD)

def hier_moe(h, w_group, b_group, w_router, b_router, w_gu, w_down):
    B, S, D = h.shape
    N = B * S
    hf = h.reshape(N, D)
    p_group = jax.nn.softmax((hf @ w_group).astype(jnp.float32) + b_group.astype(jnp.float32), axis=-1)
    g_sel = jnp.argmax(p_group, axis=-1)
    gate_g = jnp.take_along_axis(p_group, g_sel[:, None], axis=-1)
    fine = ((hf @ w_router).astype(jnp.float32) + b_router.astype(jnp.float32)
            ).reshape(N, N_GROUPS, EXPERTS_PER_GROUP)
    fine_sel = jnp.take_along_axis(fine, g_sel[:, None, None], axis=1)[:, 0]
    top_v, top_i = lax.top_k(fine_sel, TOP_K)
    gate = jax.nn.softmax(top_v, axis=-1) * gate_g
    expert = g_sel[:, None] * EXPERTS_PER_GROUP + top_i

    A = N * TOP_K
    e_flat = expert.reshape(A)
    t_flat = jnp.arange(A) // TOP_K
    w_flat = gate.reshape(A)
    order = jnp.argsort(e_flat)
    e_s, t_s, w_s = e_flat[order], t_flat[order], w_flat[order]
    counts = jnp.bincount(e_flat, length=N_EXPERTS_2)
    starts = jnp.cumsum(counts) - counts
    padded = (counts + EXPERT_BLOCK - 1) // EXPERT_BLOCK * EXPERT_BLOCK
    pad_end = jnp.cumsum(padded)
    pad_start = pad_end - padded
    dest = pad_start[e_s] + (jnp.arange(A) - starts[e_s])
    n_blocks = -(-A // EXPERT_BLOCK) + N_EXPERTS_2
    P = n_blocks * EXPERT_BLOCK
    tok_buf = jnp.full((P,), N, jnp.int32).at[dest].set(t_s.astype(jnp.int32))
    w_buf = jnp.zeros((P,), jnp.float32).at[dest].set(w_s)
    blk_expert = jnp.minimum(
        jnp.searchsorted(pad_end, jnp.arange(n_blocks) * EXPERT_BLOCK, side='right'), N_EXPERTS_2 - 1)
    x_pad = jnp.concatenate([hf, jnp.zeros((1, D), hf.dtype)], axis=0)
    xb = x_pad[tok_buf].reshape(n_blocks, EXPERT_BLOCK, D)

    def expert_block(args):
        xblk, e = args
        gt, up = jnp.split(xblk @ w_gu[e], 2, axis=-1)
        return (jax.nn.silu(gt) * up) @ w_down[e]

    yb = lax.map(expert_block, (xb, blk_expert)).reshape(P, D)
    out = jnp.zeros((N + 1, D), h.dtype).at[tok_buf].add(yb * w_buf[:, None].astype(h.dtype))
    return out[:N].reshape(B, S, D)

def second_inputs(seed: int = 0) -> dict:
    key = jax.random.key(seed)
    ks = jax.random.split(key, 32)
    f32 = jnp.float32

    def nrm(k, shape, scale):
        return jax.random.normal(k, shape, f32) * scale

    L, D = DEPTH, D_MODEL
    x = jax.random.normal(ks[0], (BATCH, SEQ, D), f32)
    offsets = jax.random.randint(ks[1], (BATCH, 1), 0, 1024, dtype=jnp.int32)
    positions = offsets + jnp.arange(SEQ, dtype=jnp.int32)[None, :]
    return {
        "x": x,
        "positions": positions,
        "mix_norm_g": 1.0 + nrm(ks[2], (L, D), 0.02),
        "w_in": nrm(ks[3], (L, D, IN_COLS_2), D ** -0.5),
        "rw_mu": jax.random.uniform(ks[4], (L, RW_COLS), f32),
        "rw_w0": jax.random.uniform(ks[5], (L, RW_DIM), f32, -6.0, -1.0),
        "rw_w_up": nrm(ks[6], (L, W_LORA, RW_DIM), 0.1 * W_LORA ** -0.5),
        "rw_a0": nrm(ks[7], (L, RW_DIM), 0.1),
        "rw_a_up": nrm(ks[8], (L, A_LORA, RW_DIM), 0.5 * A_LORA ** -0.5),
        "rw_g_up": nrm(ks[9], (L, G_LORA, RW_DIM), G_LORA ** -0.5),
        "rw_k_k": 0.85 + nrm(ks[10], (L, RW_DIM), 0.02),
        "rw_k_a": 1.0 + nrm(ks[11], (L, RW_DIM), 0.02),
        "rw_r_k": nrm(ks[12], (L, RW_HEADS, RW_HEAD_DIM), 0.1),
        "rw_gn_w": 1.0 + nrm(ks[13], (L, RW_DIM), 0.02),
        "rw_gn_b": nrm(ks[14], (L, RW_DIM), 0.02),
        "mla_g_qa": 1.0 + nrm(ks[15], (L, Q_LORA), 0.02),
        "mla_w_q_up": nrm(ks[16], (L, Q_LORA, MLA_HEADS * (QK_NOPE + QK_ROPE)), Q_LORA ** -0.5),
        "mla_g_kva": 1.0 + nrm(ks[17], (L, KV_LORA), 0.02),
        "mla_w_kv_up": nrm(ks[18], (L, KV_LORA, MLA_HEADS * (QK_NOPE + V_HEAD)), KV_LORA ** -0.5),
        "w_branch_rw": nrm(ks[19], (L, RW_DIM, D), RW_DIM ** -0.5),
        "w_branch_mla": nrm(ks[20], (L, MLA_HEADS * V_HEAD, D), (MLA_HEADS * V_HEAD) ** -0.5),
        "w_out": nrm(ks[21], (L, D, D), D ** -0.5),
        "ffn_norm_g": 1.0 + nrm(ks[22], (L, D), 0.02),
        "moe_w_group": nrm(ks[23], (L, D, N_GROUPS), D ** -0.5),
        "moe_b_group": nrm(ks[24], (L, N_GROUPS), 0.01),
        "moe_w_router": nrm(ks[25], (L, D, N_EXPERTS_2), D ** -0.5),
        "moe_b_router": nrm(ks[26], (L, N_EXPERTS_2), 0.01),
        "moe_w_gu": nrm(ks[27], (L, N_EXPERTS_2, D, 2 * D_EXPERT), D ** -0.5),
        "moe_w_down": nrm(ks[28], (L, N_EXPERTS_2, D_EXPERT, D), D_EXPERT ** -0.5),
        "final_norm_g": 1.0 + nrm(ks[29], (D,), 0.02),
    }

def second_block(x, positions, mix_norm_g, w_in, rw_mu, rw_w0, rw_w_up, rw_a0, rw_a_up, rw_g_up,
              rw_k_k, rw_k_a, rw_r_k, rw_gn_w, rw_gn_b, mla_g_qa, mla_w_q_up, mla_g_kva, mla_w_kv_up,
              w_branch_rw, w_branch_mla, w_out, ffn_norm_g, moe_w_group, moe_b_group, moe_w_router,
              moe_b_router, moe_w_gu, moe_w_down, final_norm_g):
    inv_freq = ROPE_THETA ** (-jnp.arange(0, QK_ROPE, 2, dtype=jnp.float32) / QK_ROPE)
    ang = positions.astype(jnp.float32)[..., None] * inv_freq
    cos, sin = jnp.cos(ang).astype(x.dtype), jnp.sin(ang).astype(x.dtype)

    for l in range(DEPTH):
        h = rmsnorm(x, mix_norm_g[l])
        cols = h @ w_in[l]
        c_rw = cols[..., :RW_COLS]
        c_q = cols[..., RW_COLS:RW_COLS + Q_LORA]
        c_kv = cols[..., RW_COLS + Q_LORA:RW_COLS + Q_LORA + KV_LORA]
        c_kr = cols[..., RW_COLS + Q_LORA + KV_LORA:RW_COLS + MLA_COLS]
        gate_rw = jax.nn.sigmoid(cols[..., RW_COLS + MLA_COLS:RW_COLS + MLA_COLS + D_MODEL])
        gate_mla = jax.nn.sigmoid(cols[..., RW_COLS + MLA_COLS + D_MODEL:])

        y_rw = rwkv7_mix(c_rw, rw_mu[l], rw_w0[l], rw_w_up[l], rw_a0[l], rw_a_up[l], rw_g_up[l],
                         rw_k_k[l], rw_k_a[l], rw_r_k[l], rw_gn_w[l], rw_gn_b[l])
        y_mla = mla_mix(c_q, c_kv, c_kr, cos, sin, mla_g_qa[l], mla_w_q_up[l], mla_g_kva[l], mla_w_kv_up[l])
        merged = gate_rw * (y_rw @ w_branch_rw[l]) + gate_mla * (y_mla @ w_branch_mla[l])
        x = x + merged @ w_out[l]

        h2 = rmsnorm(x, ffn_norm_g[l])
        x = x + hier_moe(h2, moe_w_group[l], moe_b_group[l], moe_w_router[l], moe_b_router[l],
                         moe_w_gu[l], moe_w_down[l])

    return rmsnorm(x, final_norm_g)


def setup_inputs(seed=0):
    out = dict(first_inputs(seed))
    for name, value in second_inputs(seed + 1).items():
        if name != "x":
            out[name + "_2"] = value
    return out


def reference(
    x, c, ctx, c_ctx, w_ada, b_ada, norm_pre_mix, norm_post_mix, norm_pre_ffn, norm_post_ffn,
    w_in, na_rpb, ssd_conv_w, ssd_conv_b, ssd_a_log_fwd, ssd_a_log_bwd, ssd_dt_bias_fwd,
    ssd_dt_bias_bwd, ssd_d_skip, ssd_norm, w_branch_na, w_branch_ssd, w_out, w_router,
    w_exp_gate, w_exp_up, w_exp_down, positions_2, mix_norm_g_2, w_in_2, rw_mu_2, rw_w0_2,
    rw_w_up_2, rw_a0_2, rw_a_up_2, rw_g_up_2, rw_k_k_2, rw_k_a_2, rw_r_k_2, rw_gn_w_2,
    rw_gn_b_2, mla_g_qa_2, mla_w_q_up_2, mla_g_kva_2, mla_w_kv_up_2, w_branch_rw_2,
    w_branch_mla_2, w_out_2, ffn_norm_g_2, moe_w_group_2, moe_b_group_2, moe_w_router_2,
    moe_b_router_2, moe_w_gu_2, moe_w_down_2, final_norm_g_2,
):
    x = first_block(
        x, c, ctx, c_ctx, w_ada, b_ada, norm_pre_mix, norm_post_mix, norm_pre_ffn,
        norm_post_ffn, w_in, na_rpb, ssd_conv_w, ssd_conv_b, ssd_a_log_fwd, ssd_a_log_bwd,
        ssd_dt_bias_fwd, ssd_dt_bias_bwd, ssd_d_skip, ssd_norm, w_branch_na, w_branch_ssd,
        w_out, w_router, w_exp_gate, w_exp_up, w_exp_down,
    )
    return second_block(
        x, positions_2, mix_norm_g_2, w_in_2, rw_mu_2, rw_w0_2, rw_w_up_2, rw_a0_2, rw_a_up_2,
        rw_g_up_2, rw_k_k_2, rw_k_a_2, rw_r_k_2, rw_gn_w_2, rw_gn_b_2, mla_g_qa_2, mla_w_q_up_2,
        mla_g_kva_2, mla_w_kv_up_2, w_branch_rw_2, w_branch_mla_2, w_out_2, ffn_norm_g_2,
        moe_w_group_2, moe_b_group_2, moe_w_router_2, moe_b_router_2, moe_w_gu_2, moe_w_down_2,
        final_norm_g_2,
    )


_drawn_inputs = setup_inputs


def setup_inputs(seed=0):
    import zlib

    import numpy as np

    out = dict(_drawn_inputs(seed))
    spreads = {}
    factors = {'norm_post_ffn': 3.226,
     'na_rpb': 6.68,
     'rw_w_up_2': 30.433,
     'rw_k_k_2': 20.048,
     'rw_k_a_2': 12.867,
     'rw_gn_w_2': 20.608,
     'rw_gn_b_2': 23.609,
     'mla_g_qa_2': 4.077,
     'mla_g_kva_2': 4.847,
     'moe_b_group_2': 17.904,
     'moe_b_router_2': 19.22,
     'final_norm_g_2': 7.696,
     'ffn_norm_g_2': 5.316}
    for name, (base, spread) in spreads.items():
        noise = np.random.default_rng([zlib.crc32(name.encode()), seed]).standard_normal(out[name].shape)
        drawn = base * np.exp(spread * noise) if base else spread * noise
        out[name] = jnp.asarray(drawn.astype(out[name].dtype))
    for name, factor in factors.items():
        out[name] = (out[name] * factor).astype(out[name].dtype)
    return out
```

```python
from contextlib import ExitStack

import numpy as np

import concourse.bass as bass
from concourse import mybir

P = 128
D = 1024
KD = D // P
L = 512
LT = L // P
CTX = 256
CT_TILES = CTX // P
EPS = 1e-6
NEG = -1e30

F32 = mybir.dt.float32
I32 = mybir.dt.int32
ALU = mybir.AluOpType
ACT = mybir.ActivationFunctionType
AX = mybir.AxisListType

HEADS = 16
HD = 64
GRID_W = 64
GRID_H = L // GRID_W
WIN_W = 16
N_DR = 2 * GRID_H - 1
N_DC = 2 * WIN_W - 1
SSD_W = 2048
SSD_H = 32
SSD_G = 4
SSD_N = 128
SSD_TAPS = 5
XBC = 3072
XBC_T = XBC // P
COL_Q, COL_K, COL_V, COL_Z = 0, 1024, 2048, 3072
COL_XBC = 5120
COL_DT = 8192
COL_GNA = 8256
COL_GSSD = 9280
RPB_PAD = 64
EC_E = 16
EC_CAP = 64
EC_FF = 2048

RW_H = 8
RW_D = 512
RW_C = 64
RW_COLS = 1792
GN_EPS = 64e-5
MLA_H = 8
MLA_QK = 96
MLA_NOPE = 64
MLA_ROPE = 32
MLA_Q = 384
MLA_KV = 256
COL_MQ = RW_COLS
COL_MKV = COL_MQ + MLA_Q
COL_MKR = COL_MKV + MLA_KV
COL_G2 = COL_MKR + MLA_ROPE
HM_G = 4
HM_E = 32
HM_PER = 8
HM_FF = 256
HM_CAP = 64


def constant_blocks():
    r = np.arange(P)
    blocks = {}
    blocks["ident"] = np.eye(P)
    blocks["ones"] = np.ones((P, P))
    blocks["eps"] = np.full((P, 1), EPS)
    blocks["gn_eps"] = np.full((P, 1), GN_EPS)
    blocks["upto"] = (r[:, None] <= r[None, :]) * 1.0
    blocks["from"] = (r[:, None] >= r[None, :]) * 1.0
    blocks["after"] = (r[:, None] > r[None, :]) * 1.0
    blocks["before"] = (r[:, None] < r[None, :]) * 1.0
    blocks["slots"] = np.tile(np.arange(1, 65, dtype=np.float32), (P, 1))
    half = HD // 4
    inv = np.float32(10000.0) ** (-np.arange(half, dtype=np.float32) / np.float32(half))
    pos = np.arange(L)
    cos, sin, swap = np.zeros((P, L)), np.zeros((P, L)), np.zeros((P, P))
    for p in range(P):
        d = p % HD
        where = pos // GRID_W if d < HD // 2 else pos % GRID_W
        ang = (where.astype(np.float32) * inv[d % half]).astype(np.float32)
        cos[p], sin[p] = np.cos(ang), np.sin(ang)
        first = (d % (HD // 2)) < half
        swap[p + half if first else p - half, p] = -1.0 if first else 1.0
    blocks["na_cos"], blocks["na_sin"], blocks["na_swap"] = cos, sin, swap
    c = np.arange(GRID_W)
    start = np.clip(c - WIN_W // 2, 0, GRID_W - WIN_W)
    ok = (c[None, :] >= start[:, None]) & (c[None, :] < start[:, None] + WIN_W)
    blocks["na_mask"] = np.tile(np.where(ok, 0.0, NEG)[::-1], (2, 1))
    blocks["na_mirror"] = np.kron(np.eye(2), np.eye(GRID_W)[::-1])
    ch, tc = r // RW_C, r % RW_C
    same = ch[:, None] == ch[None, :]
    mid = RW_C // 2 - 1
    jj, tt = tc[:, None], tc[None, :]
    blocks["rw_mid"] = same * (1.0 * ((jj > mid) & (jj <= tt)) - 1.0 * ((jj <= mid) & (jj > tt)))
    blocks["rw_midx"] = same * (1.0 * ((jj > mid) & (jj < tt)) - 1.0 * ((jj <= mid) & (jj >= tt)))
    blocks["rw_mask"] = np.concatenate([same * (jj < tt), same * (jj <= tt)], 1) * 1.0
    for lev in range(6):
        b = 2 << lev
        blocks[f"rw_lev{lev}"] = ((r[:, None] // b == r[None, :] // b) & (jj % b < b // 2) & (tt % b >= b // 2)) * 1.0
    blocks["rw_eye"] = np.concatenate([np.eye(RW_C), np.eye(RW_C)], 0)
    blocks["rw_dlo"] = np.stack([(r < RW_C) & (tc <= mid), (r < RW_C) & (tc > mid),
                                 (r >= RW_C) & (tc <= mid), (r >= RW_C) & (tc > mid)], 1) * 1.0
    swap = np.zeros((P, P))
    for p in range(MLA_ROPE // 2):
        swap[MLA_NOPE + 16 + p, MLA_NOPE + p] = -1.0
        swap[MLA_NOPE + p, MLA_NOPE + 16 + p] = 1.0
    blocks["mla_swap"] = swap
    blocks["mla_causal"] = np.where(r[None, :] <= r[:, None], 0.0, NEG)
    inv2 = np.float32(10000.0) ** (-np.arange(0, MLA_ROPE, 2, dtype=np.float32) / np.float32(MLA_ROPE))
    blocks["mla_inv"] = np.tile(inv2, (P, 1))
    blocks["idx4"] = np.tile(np.arange(HM_G), (P, 1))
    blocks["idx32"] = np.tile(np.arange(HM_E), (P, 1))
    blocks["grp32"] = np.tile(np.arange(HM_E) // HM_PER, (P, 1))
    return {n: np.asarray(b, np.float32) for n, b in blocks.items()}


def constant_offsets():
    at, out = 0, {}
    for n, b in constant_blocks().items():
        out[n] = (at, b.shape[1])
        at += b.shape[1]
    return out, at


CONST_GROUPS = {"all": ("ident", "na_cos"), "na": ("na_cos", "rw_mid"), "rw": ("rw_mid", "mla_swap"), "mla": ("mla_swap", "idx4"),
                "moe": ("idx4", None)}


class Steps:

    def __init__(self, eng, sem, start=0):
        self.eng, self.sem, self.start, self.n = eng, sem, start, 0

    def __call__(self, ins):
        self.n += 1
        ins.then_inc(self.sem, 1)
        self.eng.wait_ge(self.sem, self.start + self.n)


class Kernel:

    def __init__(self, nc, dram):
        self.nc, self.dram = nc, dram
        self.offsets, self.n_constants = constant_offsets()
        self.loaded = {}

    def const(self, name, parts=P):
        tile, a, n = self.loaded[name]
        return tile[0:parts, a:a + n]


def load_constants(k, scope, group):
    first, last = CONST_GROUPS[group]
    a = k.offsets[first][0]
    b = k.offsets[last][0] if last else k.n_constants
    tile = scope.enter_context(k.nc.sbuf_tensor(f"const_{group}", [P, b - a], F32))
    for name, (at_col, n) in k.offsets.items():
        if a <= at_col < b:
            k.loaded[name] = (tile, at_col - a, n)
    load(k, f"const_{group}", [(tile[:, :], k.dram["constants"][:, a:b])])


def stage(k, label):
    ctx = ExitStack()
    sems = []

    def retire():
        k.nc.clear_and_free_semaphores(sems)
        k.nc.all_engine_barrier(sem_only=True)

    ctx.callback(retire)

    def sb(name, shape, dt=F32):
        return ctx.enter_context(k.nc.sbuf_tensor(f"{label}_{name}", shape, dt))

    def ps(name, shape):
        return ctx.enter_context(k.nc.psum_tensor(f"{label}_{name}", shape, F32))

    def sem(name):
        sems.append(k.nc.alloc_semaphore(f"{label}_{name}"))
        return sems[-1]

    return ctx, sb, ps, sem


def load(k, label, moves):
    ctx, sb, ps, sem = stage(k, label)
    with ctx:
        moved = sem("moved")
        block = ctx.enter_context(k.nc.Block())

        @block.sync
        def _(sp):
            for dst, src in moves:
                sp.dma_start(dst, src).then_inc(moved, 16)
            sp.wait_ge(moved, 16 * len(moves))


def rows_view(x):
    return x[0].rearrange("(t p) d -> p t d", p=P)


def norm_transpose(k, label, x, nt, xT, scale_cols, shift_cols=None, xn=None):
    nc = k.nc
    ctx, sb, ps, sem = stage(k, label)
    with ctx:
        if xn is None:
            xn = sb("xn", [P, nt, D])
        square = sb("square", [P, D])
        ss = sb("ss", [P, nt])
        rstd = sb("rstd", [P, nt])
        pt = ps("pt", [P, 4, 512])
        act_step, dve_step = sem("act_step"), sem("dve_step")
        root_ready, row_ready, tile_ready, tile_free = sem("root_ready"), sem("row_ready"), sem("tile_ready"), sem("tile_free")
        block = ctx.enter_context(nc.Block())

        @block.scalar
        def _(act):
            link = Steps(act, act_step)
            for t in range(nt):
                link(act.activation(square[:, :], x[:, t, :], ACT.Square, accum_out=ss[:, t:t + 1]))
            act.activation(rstd[:, :], ss[:, :], ACT.Sqrt, scale=1.0 / D, bias=k.const("eps")).then_inc(root_ready, 1)

        @block.vector
        def _(dve):
            link = Steps(dve, dve_step)
            dve.wait_ge(root_ready, 1)
            link(dve.reciprocal(rstd[:, :], rstd[:, :]))
            for t in range(nt):
                dve.tensor_scalar(xn[:, t, :], x[:, t, :], rstd[:, t:t + 1], None, ALU.mult).then_inc(row_ready, 1)
            for j in range(KD):
                dve.wait_ge(tile_ready, j + 1)
                if shift_cols is None:
                    ins = dve.tensor_scalar(xT[:, j, :], pt[:, j % 4, 0:nt * P], scale_cols[:, j:j + 1], None, ALU.mult)
                else:
                    ins = dve.tensor_scalar(xT[:, j, :], pt[:, j % 4, 0:nt * P], scale_cols[:, j:j + 1],
                                            shift_cols[:, j:j + 1], ALU.mult, ALU.add)
                ins.then_inc(tile_free, 1)

        @block.tensor
        def _(pe):
            pe.wait_ge(row_ready, nt)
            for j in range(KD):
                if j >= 4:
                    pe.wait_ge(tile_free, j - 3)
                for t in range(nt):
                    last = pe.transpose(pt[:, j % 4, t * P:(t + 1) * P], xn[:, t, j * P:(j + 1) * P], k.const("ident"))
                last.then_inc(tile_ready, 1)


def transpose_rows(k, label, x, nt, nf, xT, scale=None):
    nc = k.nc
    ctx, sb, ps, sem = stage(k, label)
    with ctx:
        pt = ps("pt", [P, 4, 512])
        tile_ready, tile_free = sem("tile_ready"), sem("tile_free")
        block = ctx.enter_context(nc.Block())

        @block.tensor
        def _(pe):
            for j in range(nf):
                if j >= 4:
                    pe.wait_ge(tile_free, j - 3)
                for t in range(nt):
                    last = pe.transpose(pt[:, j % 4, t * P:(t + 1) * P], x[:, t, j * P:(j + 1) * P], k.const("ident"))
                last.then_inc(tile_ready, 1)

        @block.vector
        def _(dve):
            for j in range(nf):
                dve.wait_ge(tile_ready, j + 1)
                if scale is None:
                    ins = dve.tensor_copy(xT[:, j, :], pt[:, j % 4, 0:nt * P])
                else:
                    ins = dve.tensor_scalar(xT[:, j, :], pt[:, j % 4, 0:nt * P], scale[:, j:j + 1], None, ALU.mult)
                ins.then_inc(tile_free, 1)


def at(t, i):
    return t[:, bass.ds(i, 1), :].rearrange("p a n -> p (a n)")


class WeightsAhead:

    def __init__(self, k, scope, name):
        sems = []
        scope.callback(lambda: (k.nc.clear_and_free_semaphores(sems), k.nc.all_engine_barrier(sem_only=True)))
        self.k, self.name = k, name
        self.tile = scope.enter_context(k.nc.sbuf_tensor(name, [P, 2, KD * 512], F32))
        for b in range(2):
            sems.append(k.nc.alloc_semaphore(f"{name}_loaded{b}"))
        self.loaded, self.count, self.pending = sems, 0, None

    def buffer(self, b, kt, width):
        return self.tile[:, b, 0:kt * width].rearrange("p (k n) -> p k n", n=width)

    def load_first(self, sp, b, w, kt, width):
        source = w.rearrange("(k p) n -> p k n", p=P)[:, :, b * width:(b + 1) * width]
        sp.dma_start(self.buffer(b, kt, width), source).then_inc(self.loaded[b], 16)
        self.pending = (kt, width)

    def start(self, w, kt, width):
        ctx, sb, ps, sem = stage(self.k, f"{self.name}_start")
        with ctx:
            block = ctx.enter_context(self.k.nc.Block())

            @block.sync
            def _(sp):
                for b in range(2):
                    self.load_first(sp, b, w, kt, width)


def project(k, label, w, kt, width, n_chunks, groups, evacuate=None, engine="vector", link_steps=0, buffers=(), ahead=None, then=None):
    nc = k.nc
    ctx, sb, ps, sem = stage(k, label)
    with ctx:
        if ahead is None:
            tile = sb("wt", [P, 2, kt, width])
            wt = [tile[:, b] for b in range(2)]
            loaded, before, coming = [sem("loaded0"), sem("loaded1")], 0, None
        else:
            wt = [ahead.buffer(b, kt, width) for b in range(2)]
            loaded, before, coming = ahead.loaded, ahead.count, ahead.pending
        assert coming in (None, (kt, width))
        acc = ps("acc", [P, 4, 512])
        extra = [sb(n, s) for n, s in buffers]
        product_ready, product_taken = sem("product_ready"), sem("product_taken")
        out_step = sem("out_step")
        block = ctx.enter_context(nc.Block())
        w_view = w.rearrange("(k p) n -> p k n", p=P)
        pairs = n_chunks // 2
        per = len(groups(wt[0], 0))
        assert n_chunks % 2 == 0 and 2 * per % 4 == 0

        @block.sync
        def _(sp):
            if coming is None:
                for b in range(2):
                    sp.dma_start(wt[b], w_view[:, :, b * width:(b + 1) * width]).then_inc(loaded[b], 16)
            if pairs > 1:
                with sp.Fori(1, pairs) as i:
                    for b in range(2):
                        sp.wait_ge(product_ready, (2 * i + (b - 1)) * per)
                        sp.dma_start(wt[b], w_view[:, :, bass.ds((2 * i + b) * width, width)]).then_inc(loaded[b], 16)
            if then is not None:
                for b in range(2):
                    sp.wait_ge(product_ready, (n_chunks - 1 + b) * per)
                    ahead.load_first(sp, b, *then)

        @block.tensor
        def _(pe):
            with pe.Fori(0, pairs) as i:
                for b in range(2):
                    pe.wait_ge(loaded[b], 16 * i + (before + 16))
                    for g, (stat, mov, rows, cols, _) in enumerate(groups(wt[b], 2 * i + b)):
                        bank = (b * per + g) % 4
                        pe.wait_ge(product_taken, (2 * i + b) * per + (g + 1))
                        for j in range(kt):
                            last = pe.matmul(acc[0:rows, bank, 0:cols], stat(j), mov(j), start=(j == 0), stop=(j == kt - 1))
                        last.then_inc(product_ready, 1)

        def take(eng):
            eng.sem_inc(product_taken, 4)
            with eng.Fori(0, pairs) as i:
                link = Steps(eng, out_step, i * (2 * per * link_steps))
                for b in range(2):
                    for g, (_, _, rows, cols, place) in enumerate(groups(wt[b], 2 * i + b)):
                        eng.wait_ge(product_ready, (2 * i + b) * per + (g + 1))
                        product = acc[0:rows, (b * per + g) % 4, 0:cols]
                        if evacuate is not None:
                            ins = evacuate(eng, link, product, place, 2 * i + b, g, extra)
                        elif engine == "vector":
                            ins = eng.tensor_copy(place, product)
                        else:
                            ins = eng.activation(place, product, ACT.Copy)
                        ins.then_inc(product_taken, 1)
                assert link.n == 2 * per * link_steps

        if engine == "vector":
            block.vector(take)
        else:
            block.scalar(take)

    if ahead is not None:
        ahead.count += 16 * pairs
        if then is None:
            ahead.pending = None


def column_vectors(k, label, rows_dram, cols):
    nc = k.nc
    ctx, sb, ps, sem = stage(k, label)
    with ctx:
        n = sum(r.shape[0] for r in rows_dram)
        rows = sb("rows", [P, P])
        pt = ps("pt", [P, P])
        loaded, ready, taken = sem("loaded"), sem("ready"), sem("taken")
        block = ctx.enter_context(nc.Block())

        @block.sync
        def _(sp):
            a = 0
            for r in rows_dram:
                sp.dma_start(rows[a:a + r.shape[0], :], r).then_inc(loaded, 16)
                a += r.shape[0]

        @block.tensor
        def _(pe):
            pe.wait_ge(loaded, 16 * len(rows_dram))
            pe.transpose(pt[:, 0:n], rows[0:n, :], k.const("ident", n)[:, 0:n]).then_inc(ready, 1)

        @block.vector
        def _(dve):
            dve.wait_ge(ready, 1)
            dve.tensor_copy(cols[:, 0:n], pt[:, 0:n]).then_inc(taken, 1)
            dve.wait_ge(taken, 1)


V_BADA, V_PREMIX, V_POSTMIX, V_PREFFN, V_POSTFFN, V_C, V_CCTX, V_CONVB = 0, 48, 56, 64, 72, 80, 88, 96
SH1, SC1, GA1, SH2, SC2, GA2 = (KD * i for i in range(6))


def modulations(k, vec, mod, scales, gains):
    nc = k.nc
    CHUNK = 4 * P
    pairs = 6 * D // CHUNK // 2
    ctx, sb, ps, sem = stage(k, "ada")
    with ctx:
        cs = sb("silu", [P, KD, 32])
        wt = sb("wt", [P, 2, KD, CHUNK])
        rows = sb("rows", [P, 2, P])
        acc, pt = ps("acc", [P, 2, 512]), ps("pt", [P, 2, 512])
        loaded = [sem("loaded0"), sem("loaded1")]
        cleared, silued, product_ready, rows_ready, flipped, taken = (sem(x) for x in ("cleared", "silued", "product_ready", "rows_ready", "flipped", "taken"))
        block = ctx.enter_context(nc.Block())
        w_view = k.dram["w_ada"][0].rearrange("(k p) n -> p k n", p=P)

        @block.sync
        def _(sp):
            with sp.Fori(0, pairs) as i:
                for b in range(2):
                    sp.wait_ge(product_ready, 2 * i + (b + 1))
                    sp.dma_start(wt[:, b], w_view[:, :, bass.ds((2 * i + b) * CHUNK, CHUNK)]).then_inc(loaded[b], 16)

        @block.scalar
        def _(act):
            act.wait_ge(cleared, 1)
            act.activation(cs[:, :, 0], vec[:, V_C:V_C + KD], ACT.Silu).then_inc(silued, 1)
            act.activation(cs[:, :, 1], vec[:, V_CCTX:V_CCTX + KD], ACT.Silu).then_inc(silued, 1)

        @block.tensor
        def _(pe):
            pe.sem_inc(product_ready, 2)
            pe.wait_ge(silued, 2)
            with pe.Fori(0, pairs) as i:
                for b in range(2):
                    pe.wait_ge(loaded[b], 16 * i + 16)
                    pe.wait_ge(rows_ready, 2 * i + (b + 1))
                    for j in range(KD):
                        for q in range(4):
                            last = pe.matmul(acc[q * 32:(q + 1) * 32, b, 0:P], cs[:, j, :], wt[:, b, j, q * P:(q + 1) * P],
                                             start=(j == 0), stop=(j == KD - 1))
                    last.then_inc(product_ready, 1)
                    pe.wait_ge(rows_ready, 2 * i + (b + 3))
                    pe.wait_ge(taken, 2 * i + (b + 1))
                    pe.transpose(pt[:, b, 0:P], rows[:, b, :], k.const("ident")).then_inc(flipped, 1)

        @block.vector
        def _(dve):
            dve.memset(cs[:, :, :], 0.0).then_inc(cleared, 1)
            dve.sem_inc(rows_ready, 2)
            dve.sem_inc(taken, 2)
            with dve.Fori(0, pairs) as i:
                for b in range(2):
                    dve.wait_ge(product_ready, 2 * i + (b + 3))
                    dve.tensor_copy(rows[:, b, :], acc[:, b, 0:P]).then_inc(rows_ready, 1)
                    dve.wait_ge(flipped, 2 * i + (b + 1))
                    dve.tensor_copy(mod[:, bass.ds(8 * i + 4 * b, 4), :],
                                    pt[:, b, 0:P].rearrange("p (q n) -> p q n", n=32)[:, :, 0:2]).then_inc(taken, 1)

    ctx, sb, ps, sem = stage(k, "ada_b")
    with ctx:
        step = sem("step")
        block = ctx.enter_context(nc.Block())

        @block.vector
        def _(dve):
            link = Steps(dve, step)
            link(dve.tensor_tensor(mod[:, :, :], mod[:, :, :],
                                   vec[:, V_BADA:V_BADA + 48].unsqueeze(2).to_broadcast([P, 48, 2]), ALU.add))
            for i, (sc, who, gain) in enumerate(((SC1, 0, V_PREMIX), (SC1, 1, V_PREMIX), (SC2, 0, V_PREFFN))):
                link(dve.scalar_tensor_tensor(scales[:, i * KD:(i + 1) * KD], mod[:, sc:sc + KD, who], 1.0,
                                              vec[:, gain:gain + KD], ALU.add, ALU.mult))
            for i, (ga, gain) in enumerate(((GA1, V_POSTMIX), (GA2, V_POSTFFN))):
                link(dve.tensor_tensor(gains[:, i, :], mod[:, ga:ga + KD, 0], vec[:, gain:gain + KD], ALU.mult))


def spread_columns(k, label, cols, rows):
    nc = k.nc
    ctx, sb, ps, sem = stage(k, label)
    with ctx:
        diag = sb("diag", [P, KD, P])
        bank = ps("bank", [P, 2, 512])
        diag_ready, rows_ready, taken = sem("diag_ready"), sem("rows_ready"), sem("taken")
        block = ctx.enter_context(nc.Block())

        @block.vector
        def _(dve):
            for j in range(KD):
                dve.tensor_scalar(diag[:, j, :], k.const("ident"), cols[:, j:j + 1], None, ALU.mult).then_inc(diag_ready, 1)
            dve.wait_ge(rows_ready, 1)
            dve.tensor_copy(rows, bank[:, :, :].rearrange("p b n -> p (b n)")).then_inc(taken, 1)
            dve.wait_ge(taken, 1)

        @block.tensor
        def _(pe):
            pe.wait_ge(diag_ready, KD)
            for j in range(KD):
                last = pe.matmul(bank[:, j // 4, (j % 4) * P:(j % 4 + 1) * P], k.const("ones"), diag[:, j, :], start=True, stop=True)
            last.then_inc(rows_ready, 1)


def rotate(k, q, key):
    nc = k.nc
    ctx, sb, ps, sem = stage(k, "rope")
    jobs = [(x, j) for j in range(KD) for x in (q, key)]
    with ctx:
        turned = sb("turned", [P, 2, L])
        bank = ps("bank", [P, 4, 512])
        swapped, turned_ready, scaled, done = sem("swapped"), sem("turned_ready"), sem("scaled"), sem("done")
        block = ctx.enter_context(nc.Block())

        @block.tensor
        def _(pe):
            for n, (x, j) in enumerate(jobs):
                if n >= 4:
                    pe.wait_ge(turned_ready, n - 3)
                pe.matmul(bank[:, n % 4, :], k.const("na_swap"), x[:, j, :], start=True, stop=True).then_inc(swapped, 1)

        @block.gpsimd
        def _(pool):
            for n, (x, j) in enumerate(jobs):
                pool.wait_ge(swapped, n + 1)
                pool.tensor_tensor(x[:, j, :], x[:, j, :], k.const("na_cos"), ALU.mult).then_inc(scaled, 1)

        @block.vector
        def _(dve):
            def add(n):
                x, j = jobs[n]
                dve.wait_ge(turned_ready, n + 1)
                dve.wait_ge(scaled, n + 1)
                dve.tensor_tensor(x[:, j, :], x[:, j, :], turned[:, n % 2, :], ALU.add).then_inc(done, 1)

            for n, (x, j) in enumerate(jobs):
                dve.wait_ge(swapped, n + 1)
                if n >= 2:
                    dve.wait_ge(done, n - 1)
                dve.tensor_tensor(turned[:, n % 2, :], bank[:, n % 4, :], k.const("na_sin"), ALU.mult).then_inc(turned_ready, 1)
                if n:
                    add(n - 1)
            add(len(jobs) - 1)
            dve.wait_ge(done, len(jobs))


def neighbourhood_attention(k, q, key, kc, v, vc, o):
    nc = k.nc
    ctx, sb, ps, sem = stage(k, "na")
    TURN = 4
    TURNS = HEADS // TURN
    N_KEY = L + CTX
    KB = N_KEY // P
    UNITS = TURN * LT
    with ctx:
        bias = sb("bias", [P, HEADS, 14 * GRID_W])
        qm = sb("qm", [P, TURN, L])
        p = sb("p", [P, 2, N_KEY])
        pT = sb("pT", [P, 2, N_KEY])
        top, total, inv = sb("top", [P, 2]), sb("total", [P, 2]), sb("inv", [P, 2])
        score = ps("score", [P, 2, 1024])
        flip = ps("flip", [P, 1024])
        out = ps("out", [P, 2, 512])
        bias_loaded = [sem(f"bias_loaded{i}") for i in range(TURNS)]
        masked, split, scored, exped = sem("masked"), sem("split"), sem("scored"), sem("exped")
        zeroed, topped, flipped, flip_taken = sem("zeroed"), sem("topped"), sem("flipped"), sem("flip_taken")
        valued, normed, dve_step = sem("valued"), sem("normed"), sem("dve_step")
        block = ctx.enter_context(nc.Block())
        mask = k.const("na_mask").unsqueeze(1).to_broadcast([P, 14, GRID_W])

        @block.sync
        def _(sp):
            table = k.dram["rpb_padded"]
            for h in range(HEADS):
                for half in range(2):
                    first = RPB_PAD + h * N_DR * N_DC + (1 - half) * N_DC + WIN_W - GRID_W
                    src = bass.AP(tensor=table.tensor, offset=first, ap=[[1, GRID_W], [N_DC, 14], [1, GRID_W]])
                    dst = bias[half * GRID_W:(half + 1) * GRID_W, h, :].rearrange("p (m c) -> p m c", c=GRID_W)
                    sp.dma_start(dst, src).then_inc(bias_loaded[h // TURN], 16)

        @block.gpsimd
        def _(pool):
            for i in range(TURNS):
                pool.wait_ge(bias_loaded[i], 16 * 2 * TURN)
                for h in range(TURN * i, TURN * (i + 1)):
                    b = bias[:, h, :].rearrange("p (m c) -> p m c", c=GRID_W)
                    pool.tensor_tensor(b, b, mask, ALU.add).then_inc(masked, 1)

        @block.tensor
        def _(pe):
            pe.sem_inc(scored, 1)
            with pe.Fori(0, TURNS) as i:
                def scores(u):
                    hp, t = u // LT, u % LT
                    pair = TURN // 2 * i + hp // 2
                    if t == 0:
                        pe.wait_ge(masked, TURN * i + (hp + 1))
                        pe.wait_ge(split, TURN * i + (hp + 1))
                    if u >= 2:
                        pe.wait_ge(exped, UNITS * i + (u - 1))
                    queries = qm[:, hp, t * P:(t + 1) * P]
                    at_dr = (GRID_H - 2 - 2 * t) * GRID_W
                    pe.matmul(score[:, u % 2, 0:L], k.const("na_mirror"), at(bias, TURN * i + hp)[:, at_dr:at_dr + L], start=True, stop=False)
                    pe.matmul(score[:, u % 2, 0:L], queries, at(key, pair), start=False, stop=True)
                    pe.matmul(score[:, u % 2, L:N_KEY], queries, at(kc, pair), start=True, stop=True).then_inc(scored, 1)

                def turn(u):
                    pe.wait_ge(exped, UNITS * i + (u + 1))
                    pe.wait_ge(flip_taken, 2 * UNITS * i + (2 * u + 1))
                    for j in range(KB):
                        last = pe.transpose(flip[:, j * P:(j + 1) * P], p[:, u % 2, j * P:(j + 1) * P], k.const("ident"))
                    last.then_inc(flipped, 1)

                def values(u):
                    hp, b = u // LT, u % 2
                    pe.wait_ge(flip_taken, 2 * UNITS * i + (2 * u + 3))
                    if u >= 2:
                        pe.wait_ge(normed, UNITS * i + (u - 1))
                    head = TURN * i + hp
                    for j in range(KB):
                        rows = v[:, j, bass.ds(head * HD, HD)] if j < LT else vc[:, j - LT, bass.ds(head * HD, HD)]
                        last = pe.matmul(out[:, b, 0:HD], pT[:, b, j * P:(j + 1) * P], rows, start=(j == 0), stop=(j == KB - 1))
                    last.then_inc(valued, 1)

                scores(0)
                scores(1)
                for u in range(UNITS):
                    turn(u)
                    if u + 2 < UNITS:
                        scores(u + 2)
                    values(u)

        @block.scalar
        def _(act):
            act.preload_act_table(ACT.Exp)
            act.sem_inc(flip_taken, 1)
            with act.Fori(0, TURNS) as i:
                act.wait_ge(scored, UNITS * i + 1)
                act.wait_ge(zeroed, 1)
                for hp in range(TURN):
                    d = slice((hp % 2) * HD, (hp % 2 + 1) * HD)
                    act.activation(qm[d, hp, :], at(q, TURN // 2 * i + hp // 2)[d, :], ACT.Copy, scale=HD ** -0.5).then_inc(split, 1)

                def weights(u):
                    b = u % 2
                    act.wait_ge(topped, UNITS * i + (u + 1))
                    act.activation(p[:, b, :], score[:, b, 0:N_KEY], ACT.Exp, bias=top[:, b:b + 1],
                                   accum_out=total[:, b:b + 1]).then_inc(exped, 1)

                weights(0)
                weights(1)
                for u in range(UNITS):
                    act.wait_ge(flipped, UNITS * i + (u + 1))
                    act.activation(pT[:, u % 2, L:N_KEY], flip[:, L:N_KEY], ACT.Copy).then_inc(flip_taken, 1)
                    if u + 2 < UNITS:
                        weights(u + 2)

        @block.vector
        def _(dve):
            steps = UNITS * 2
            dve.memset(qm[:, :, :], 0.0).then_inc(zeroed, 1)
            with dve.Fori(0, TURNS) as i:
                link = Steps(dve, dve_step, steps * i)

                def highest(u):
                    b = u % 2
                    dve.wait_ge(scored, UNITS * i + (u + 2))
                    if u >= 2:
                        dve.wait_ge(exped, UNITS * i + (u - 1))
                    link(dve.tensor_reduce(top[:, b:b + 1], score[:, b, 0:N_KEY], AX.X, ALU.max))
                    dve.tensor_scalar(top[:, b:b + 1], top[:, b:b + 1], -1.0, None, ALU.mult).then_inc(topped, 1)

                highest(0)
                highest(1)
                for u in range(UNITS):
                    hp, t, b = u // LT, u % LT, u % 2
                    dve.wait_ge(flipped, UNITS * i + (u + 1))
                    dve.tensor_copy(pT[:, b, 0:L], flip[:, 0:L]).then_inc(flip_taken, 1)
                    link(dve.reciprocal(inv[:, b:b + 1], total[:, b:b + 1]))
                    if u + 2 < UNITS:
                        highest(u + 2)
                    dve.wait_ge(valued, UNITS * i + (u + 1))
                    dve.tensor_scalar(o[:, t, bass.ds((TURN * i + hp) * HD, HD)], out[:, b, 0:HD], inv[:, b:b + 1], None,
                                      ALU.mult).then_inc(normed, 1)
                assert link.n == steps


def conv_silu(k, label, hT, hcT, pads, tile0, n_tiles, vec, taps, xw, xcw, targets, ahead, then_tile=None):
    nc = k.nc
    pad, padc, conv = pads

    def groups(wt, c):
        out = []
        for m in range(2):
            w = lambda j, m=m: wt[:, j, m * P:(m + 1) * P]
            out.append((w, lambda j: hT[:, j, :], P, L, at(xw, 2 * c + m)))
            out.append((w, lambda j: hcT[:, j, :], P, CTX, at(xcw, 2 * c + m)))
        return out

    def evacuate(dve, link, product, place, c, g, extra):
        n = L if g % 2 == 0 else CTX
        padded = (pad if g % 2 == 0 else padc)[:, 0:n + SSD_TAPS - 1]
        tile = 2 * c + (tile0 + g // 2)
        link(dve.tensor_copy(padded[:, 2:2 + n], product))
        for tap in range(SSD_TAPS):
            w = taps[:, bass.ds(tile + tap * XBC_T, 1)]
            if tap == 0:
                link(dve.tensor_scalar(conv[:, 0:n], padded[:, 0:n], w, None, ALU.mult))
            else:
                ins = dve.scalar_tensor_tensor(place if tap == SSD_TAPS - 1 else conv[:, 0:n], padded[:, tap:tap + n], w,
                                               conv[:, 0:n], ALU.mult, ALU.add)
                if tap < SSD_TAPS - 1:
                    link(ins)
        return ins

    def weights(tile):
        return k.dram["w_in"][0][:, COL_XBC + tile * P:COL_XBC + XBC]

    project(k, label, weights(tile0), KD, 256, n_tiles // 2, groups, evacuate, link_steps=SSD_TAPS, ahead=ahead,
            then=None if then_tile is None else (weights(then_tile), KD, 256))

    ctx, sb, ps, sem = stage(k, label + "_t")
    with ctx:
        bank = ps("bank", [P, 4, 512])
        silued, flipped, taken = sem("silued"), sem("flipped"), sem("taken")
        block = ctx.enter_context(nc.Block())
        jobs = []
        for tile, rows, rows_c, col in targets:
            if rows is not None:
                jobs.append((tile, xw, LT, rows, col))
            if rows_c is not None:
                jobs.append((tile, xcw, CT_TILES, rows_c, col))

        @block.scalar
        def _(act):
            for j in range(n_tiles):
                b = vec[:, V_CONVB + tile0 + j:V_CONVB + tile0 + j + 1]
                act.activation(xw[:, j, :], xw[:, j, :], ACT.Silu, bias=b).then_inc(silued, 1)
                act.activation(xcw[:, j, :], xcw[:, j, :], ACT.Silu, bias=b).then_inc(silued, 1)
            act.wait_ge(silued, 2 * n_tiles)

        @block.tensor
        def _(pe):
            for n, (tile, src, nt, rows, col) in enumerate(jobs):
                pe.wait_ge(silued, 2 * (tile + 1))
                if n >= 4:
                    pe.wait_ge(taken, n - 3)
                for t in range(nt):
                    last = pe.transpose(bank[:, n % 4, t * P:(t + 1) * P], src[:, tile, t * P:(t + 1) * P], k.const("ident"))
                last.then_inc(flipped, 1)

        @block.vector
        def _(dve):
            for n, (tile, src, nt, rows, col) in enumerate(jobs):
                dve.wait_ge(flipped, n + 1)
                dve.tensor_copy(rows[:, :, col:col + P],
                                bank[:, n % 4, 0:nt * P].rearrange("p (t c) -> p t c", c=P)).then_inc(taken, 1)


N_SEG = LT + CT_TILES


def ssd_steps(k, hT, hcT, dt, a, dec):
    nc = k.nc
    ctx, sb, ps, sem = stage(k, "dt")
    n = N_SEG * 64
    with ctx:
        w = sb("w", [P, KD, 64])
        bias, a_log = sb("bias", [P, 64]), sb("a_log", [P, 64])
        raw, pos, u, w1, ln, eq, den = (sb(x, [P, n]) for x in ("raw", "pos", "u", "w1", "ln", "eq", "den"))
        prod = ps("prod", [P, 512])
        sums = ps("sums", [P, 3, 512])
        loaded, ready, step, act_step = sem("loaded"), sem("ready"), sem("step"), sem("act_step")
        exp_in, exp_out, ln_in, a_ready, sums_ready, done = (sem(x) for x in ("exp_in", "exp_out", "ln_in", "a_ready", "sums_ready", "done"))
        block = ctx.enter_context(nc.Block())

        @block.sync
        def _(sp):
            sp.dma_start(w[:, :, :], k.dram["w_in"][0][:, COL_DT:COL_DT + 64].rearrange("(k p) n -> p k n", p=P)).then_inc(loaded, 16)
            for i, d in enumerate(("fwd", "bwd")):
                sp.dma_start(bias[:, 32 * i:32 * i + 32], k.dram["ssd_dt_bias_" + d][0:1, :].to_broadcast([P, 32])).then_inc(loaded, 16)
                sp.dma_start(a_log[:, 32 * i:32 * i + 32], k.dram["ssd_a_log_" + d][0:1, :].to_broadcast([P, 32])).then_inc(loaded, 16)

        @block.tensor
        def _(pe):
            pe.wait_ge(loaded, 16 * 5)
            for t in range(N_SEG):
                src, c = (hT, t) if t < LT else (hcT, t - LT)
                for j in range(KD):
                    last = pe.matmul(prod[:, t * 64:(t + 1) * 64], src[:, j, c * P:(c + 1) * P], w[:, j, :],
                                     start=(j == 0), stop=(j == KD - 1))
            last.then_inc(ready, 1)
            pe.wait_ge(a_ready, 1)
            for d in range(2):
                for t in range(N_SEG):
                    m = d * N_SEG + t
                    for i, name in enumerate((("upto", "after", "ones"), ("from", "before", "ones"))[d]):
                        c = (m % 4) * 96 + i * 32
                        last = pe.matmul(sums[:, m // 4, c:c + 32], k.const(name), a[:, t, d * 32:(d + 1) * 32],
                                         start=True, stop=True)
            last.then_inc(sums_ready, 1)

        @block.scalar
        def _(act):
            act.wait_ge(loaded, 16 * 5)
            act.activation(a_log[:, :], a_log[:, :], ACT.Exp).then_inc(exp_out, 1)
            act.wait_ge(exp_in, 1)
            act.activation(u[:, :], u[:, :], ACT.Exp).then_inc(exp_out, 1)
            act.wait_ge(ln_in, 1)
            act.activation(ln[:, :], w1[:, :], ACT.Ln).then_inc(exp_out, 1)
            act.wait_ge(sums_ready, 1)
            act.activation(dec[:, :, :].rearrange("p (b m) n -> p b (m n)", b=3), sums[:, :, 0:384], ACT.Exp).then_inc(done, 1)
            act.wait_ge(done, 1)

        @block.vector
        def _(dve):
            link = Steps(dve, step)
            dve.wait_ge(ready, 1)
            link(dve.tensor_tensor(raw[:, :].rearrange("p (t h) -> p t h", h=64), prod[:, 0:n].rearrange("p (t h) -> p t h", h=64),
                                   bias[:, :].unsqueeze(1).to_broadcast([P, N_SEG, 64]), ALU.add))
            link(dve.tensor_scalar(pos[:, :], raw[:, :], 0.0, None, ALU.max))
            dve.scalar_tensor_tensor(u[:, :], raw[:, :], -1.0, raw[:, :], ALU.mult, ALU.min).then_inc(exp_in, 1)
            dve.wait_ge(exp_out, 2)
            dve.tensor_scalar(w1[:, :], u[:, :], 1.0, None, ALU.add).then_inc(ln_in, 1)
            dve.wait_ge(ln_in, 1)
            link(dve.tensor_scalar(den[:, :], w1[:, :], -1.0, None, ALU.add))
            link(dve.tensor_scalar(eq[:, :], den[:, :], 0.0, None, ALU.is_equal))
            link(dve.tensor_tensor(den[:, :], den[:, :], eq[:, :], ALU.add))
            link(dve.reciprocal(den[:, :], den[:, :]))
            link(dve.tensor_tensor(den[:, :], den[:, :], u[:, :], ALU.mult))
            dve.wait_ge(exp_out, 3)
            link(dve.tensor_tensor(ln[:, :], ln[:, :], eq[:, :], ALU.add))
            link(dve.tensor_tensor(ln[:, :], ln[:, :], den[:, :], ALU.mult))
            link(dve.tensor_tensor(dt[:, :, :].rearrange("p t h -> p (t h)"), ln[:, :], pos[:, :], ALU.add))
            link(dve.tensor_tensor(a[:, :, :], dt[:, :, :], a_log[:, :].unsqueeze(1).to_broadcast([P, N_SEG, 64]), ALU.mult))
            dve.tensor_scalar(a[:, :, :], a[:, :, :], -1.0, None, ALU.mult).then_inc(a_ready, 1)


def ssd_scan(k, xs, xsc, bT, cT, b_rows, bc_rows, dt, a, dec, y):
    nc = k.nc
    ctx, sb, ps, sem = stage(k, "ssd")
    HG = SSD_H // SSD_G
    GW = HG * 64
    units = []
    for s in range(N_SEG):
        for d in range(2):
            main = s >= CT_TILES
            c = s - CT_TILES if main else s
            c = c if d == 0 else (LT if main else CT_TILES) - 1 - c
            for g in range(SSD_G):
                units.append((main, d, c, g))
    mains = [n for n, u in enumerate(units) if u[0]]
    chain = 2 * SSD_G
    with ctx:
        state = sb("state", [P, 2, SSD_G, GW])
        xd, xde = sb("xd", [P, 2, GW]), sb("xde", [P, 2, GW])
        seg_in = sb("seg_in", [P, 2, HG, P])
        lx = sb("lx", [P, 2, HG, P])
        cbm = sb("cbm", [P, 2, P])
        off = sb("off", [P, 2, GW])
        seg = ps("seg", [P, 2, 512])
        cb, yd, yo, st = ps("cb", [P, 512]), ps("yd", [P, 512]), ps("yo", [P, 512]), ps("st", [P, 512])
        inputs_ready, seg_built, seg_ready, exped, mixed = (sem(x) for x in ("inputs_ready", "seg_built", "seg_ready", "exped", "mixed"))
        state_ready, state_done, off_ready, diag_ready, y_done = (sem(x) for x in ("state_ready", "state_done", "off_ready", "diag_ready", "y_done"))
        masked, pool_step, dve_step = sem("masked"), sem("pool_step"), sem("dve_step")
        block = ctx.enter_context(nc.Block())

        def tile(u):
            return u[2] if u[0] else LT + u[2]

        def spread(ap, n):
            return ap.unsqueeze(2).to_broadcast([P, HG, n])

        @block.gpsimd
        def _(pool):
            link = Steps(pool, pool_step)
            m = 0
            for n, u in enumerate(units):
                main, d, c, g = u
                x = (xs if main else xsc)[:, c, g * GW:(g + 1) * GW].rearrange("p (h e) -> p h e", h=HG)
                hs = d * SSD_H + g * HG
                if main:
                    if m >= 2:
                        pool.wait_ge(seg_ready, m - 1)
                    cum = k.const("upto" if d == 0 else "from")
                    pool.tensor_tensor(seg_in[:, m % 2], cum.unsqueeze(1).to_broadcast([P, HG, P]),
                                       spread(a[:, tile(u), hs:hs + HG], P), ALU.mult).then_inc(seg_built, 1)
                if n >= 2:
                    pool.wait_ge(state_ready, n - 1)
                    if n - 2 in mains:
                        pool.wait_ge(diag_ready, mains.index(n - 2) + 1)
                link(pool.tensor_tensor(xd[:, n % 2].rearrange("p (h e) -> p h e", h=HG), x,
                                        spread(dt[:, tile(u), hs:hs + HG], 64), ALU.mult))
                e2 = dec[:, d * N_SEG + tile(u), 32 + g * HG:32 + (g + 1) * HG]
                pool.tensor_tensor(xde[:, n % 2].rearrange("p (h e) -> p h e", h=HG),
                                   xd[:, n % 2].rearrange("p (h e) -> p h e", h=HG), spread(e2, 64),
                                   ALU.mult).then_inc(inputs_ready, 1)
                m += main

        @block.tensor
        def _(pe):
            def segments(m):
                _, d, c, g = units[mains[m]]
                pe.wait_ge(seg_built, m + 1)
                if m >= 1:
                    pe.wait_ge(exped, m)
                    pe.wait_ge(masked, m)
                for h in range(2):
                    pe.matmul(seg[:, h, :], k.const("after" if d == 0 else "before"),
                              seg_in[:, m % 2, 4 * h:4 * h + 4].rearrange("p h l -> p (h l)"), start=True, stop=True)
                pe.matmul(cb[:, 0:P], bT[:, g, c * P:(c + 1) * P], cT[:, g, c * P:(c + 1) * P], start=True,
                          stop=True).then_inc(seg_ready, 1)

            m = 0
            for n, u in enumerate(units):
                main, d, c, g = u
                if n == mains[0]:
                    segments(0)
                pe.wait_ge(inputs_ready, n + 1)
                if n >= 1:
                    pe.wait_ge(state_done, n)
                pe.matmul(st[:, :], (b_rows if main else bc_rows)[:, c, g * P:(g + 1) * P], xde[:, n % 2, :], start=True,
                          stop=True).then_inc(state_ready, 1)
                if main:
                    if m >= 1:
                        pe.wait_ge(y_done, m)
                    pe.matmul(yo[:, :], cT[:, g, c * P:(c + 1) * P], state[:, d, g, :], start=True, stop=True).then_inc(off_ready, 1)
                    if m + 1 < len(mains):
                        segments(m + 1)
                    pe.wait_ge(mixed, m + 1)
                    for h in range(HG):
                        last = pe.matmul(yd[:, h * 64:(h + 1) * 64], lx[:, m % 2, h, :], xd[:, n % 2, h * 64:(h + 1) * 64],
                                         start=True, stop=True)
                    last.then_inc(diag_ready, 1)
                    m += 1

        @block.scalar
        def _(act):
            for m in range(len(mains)):
                act.wait_ge(seg_ready, m + 1)
                if m >= 2:
                    act.wait_ge(diag_ready, m - 1)
                act.activation(lx[:, m % 2].rearrange("p (b h) l -> p b (h l)", b=2), seg[:, :, :], ACT.Exp).then_inc(exped, 1)

        @block.vector
        def _(dve):
            link = Steps(dve, dve_step)
            m = 0
            for n, u in enumerate(units):
                main, d, c, g = u
                t = d * N_SEG + tile(u)
                if main:
                    dve.wait_ge(seg_ready, m + 1)
                    dve.tensor_tensor(cbm[:, m % 2, :], cb[:, 0:P], k.const("upto" if d == 0 else "from"),
                                      ALU.mult).then_inc(masked, 1)
                    dve.wait_ge(masked, m + 1)
                    dve.wait_ge(exped, m + 1)
                    dve.tensor_tensor(lx[:, m % 2], lx[:, m % 2], cbm[:, m % 2, :].unsqueeze(1).to_broadcast([P, HG, P]),
                                      ALU.mult).then_inc(mixed, 1)
                    dve.wait_ge(off_ready, m + 1)
                dve.wait_ge(state_ready, n + 1)
                if n < chain:
                    dve.tensor_copy(state[:, d, g, :], st[:, :]).then_inc(state_done, 1)
                else:
                    e3 = dec[:, t, 64 + g * HG:64 + (g + 1) * HG]
                    sv = state[:, d, g, :].rearrange("p (h e) -> p h e", h=HG)
                    link(dve.tensor_tensor(sv, sv, spread(e3, 64), ALU.mult))
                    dve.tensor_tensor(state[:, d, g, :], state[:, d, g, :], st[:, :], ALU.add).then_inc(state_done, 1)
                if main:
                    e1 = dec[:, t, g * HG:(g + 1) * HG]
                    link(dve.tensor_tensor(off[:, m % 2].rearrange("p (h e) -> p h e", h=HG),
                                           yo[:, :].rearrange("p (h e) -> p h e", h=HG), spread(e1, 64), ALU.mult))
                    dve.wait_ge(diag_ready, m + 1)
                    first = (c < LT // 2) == (d == 0)
                    yv = y[:, c, g * GW:(g + 1) * GW]
                    if first:
                        dve.tensor_tensor(yv, off[:, m % 2], yd[:, :], ALU.add).then_inc(y_done, 1)
                    else:
                        link(dve.tensor_tensor(off[:, m % 2], off[:, m % 2], yd[:, :], ALU.add))
                        dve.tensor_tensor(yv, yv, off[:, m % 2], ALU.add).then_inc(y_done, 1)
                    m += 1
                dve.wait_ge(state_done, n + 1)
            dve.wait_ge(y_done, m)


def ssd_gate_norm(k, y, xs, z, skip):
    nc = k.nc
    ctx, sb, ps, sem = stage(k, "gatenorm")
    GW = SSD_W // SSD_G
    n = LT * SSD_G
    with ctx:
        skipped = sb("skipped", [P, 2, GW])
        square = sb("square", [P, GW])
        ss, rstd = sb("ss", [P, n]), sb("rstd", [P, n])
        skipped_ready, gated, squared, step, act_step, normed = (sem(x) for x in ("skipped_ready", "gated", "squared", "step", "act_step", "normed"))
        block = ctx.enter_context(nc.Block())
        pieces = [(i, t, slice(g * GW, (g + 1) * GW), g) for i, (t, g) in enumerate((t, g) for t in range(LT) for g in range(SSD_G))]

        @block.gpsimd
        def _(pool):
            for i, t, cols, g in pieces:
                if i >= 2:
                    pool.wait_ge(gated, i - 1)
                pool.tensor_tensor(skipped[:, i % 2].rearrange("p (h e) -> p h e", e=64),
                                   xs[:, t, cols].rearrange("p (h e) -> p h e", e=64),
                                   skip[:, g * 8:(g + 1) * 8].unsqueeze(2).to_broadcast([P, 8, 64]), ALU.mult).then_inc(skipped_ready, 1)

        @block.scalar
        def _(act):
            link = Steps(act, act_step)
            for i, t, cols, g in pieces:
                act.wait_ge(gated, i + 1)
                link(act.activation(square[:, :], y[:, t, cols], ACT.Square, accum_out=ss[:, i:i + 1]))
            act.activation(rstd[:, :], ss[:, :], ACT.Sqrt, scale=1.0 / GW, bias=k.const("eps")).then_inc(squared, 1)

        @block.vector
        def _(dve):
            link = Steps(dve, step)
            for i, t, cols, g in pieces:
                dve.wait_ge(skipped_ready, i + 1)
                link(dve.tensor_tensor(y[:, t, cols], y[:, t, cols], skipped[:, i % 2], ALU.add))
                dve.tensor_tensor(y[:, t, cols], y[:, t, cols], z[:, t, cols], ALU.mult).then_inc(gated, 1)
            dve.wait_ge(squared, 1)
            link(dve.reciprocal(rstd[:, :], rstd[:, :]))
            for i, t, cols, g in pieces:
                dve.tensor_scalar(y[:, t, cols], y[:, t, cols], rstd[:, i:i + 1], None, ALU.mult).then_inc(normed, 1)
            dve.wait_ge(normed, n)


def gated_branch(k, label, w_gate, hT, w, feats, inT, uT, add, ahead, then=None):
    nc = k.nc
    with ExitStack() as outer:
        gate = outer.enter_context(nc.sbuf_tensor(f"{label}_gate", [P, KD, L], F32))

        def gate_groups(wt, c):
            return [(lambda j, m=m: wt[:, j, m * P:(m + 1) * P], lambda j: hT[:, j, :], P, L, at(gate, 4 * c + m)) for m in range(4)]

        def sigmoid(act, link, product, place, c, g, extra):
            return act.activation(place, product, ACT.Sigmoid)

        width = min(512, KD * 512 // feats)
        project(k, label + "_g", w_gate, KD, 512, 2, gate_groups, sigmoid, engine="scalar", ahead=ahead, then=(w, feats, width))
        per = width // P

        def groups(wt, c):
            return [(lambda j, m=m: wt[:, j, m * P:(m + 1) * P], lambda j: inT[:, j, :], P, L, at(uT, per * c + m)) for m in range(per)]

        def merge(dve, link, product, place, c, g, extra):
            s = at(gate, per * c + g)
            if not add:
                return dve.tensor_tensor(place, product, s, ALU.mult)
            link(dve.tensor_tensor(s, product, s, ALU.mult))
            return dve.tensor_tensor(place, place, s, ALU.add)

        project(k, label + "_b", w, feats, width, D // width, groups, merge, link_steps=1 if add else 0, ahead=ahead, then=then)


def project_rows(k, label, w, kt, xT, out, n_chunks, width=512, ahead=None, then=None):
    def groups(wt, c):
        return [(lambda j, t=t: xT[:, j, t * P:(t + 1) * P], lambda j: wt[:, j, :], P, width, out[:, t, bass.ds(c * width, width)])
                for t in range(LT)]

    project(k, label, w, kt, width, n_chunks, groups, ahead=ahead, then=then)


def add_normed(k, label, x, branch, gain_rows):
    nc = k.nc
    ctx, sb, ps, sem = stage(k, label)
    with ctx:
        square = sb("square", [P, D])
        ss, rstd = sb("ss", [P, LT]), sb("rstd", [P, LT])
        root_ready, act_step, step = sem("root_ready"), sem("act_step"), sem("step")
        block = ctx.enter_context(nc.Block())

        @block.scalar
        def _(act):
            link = Steps(act, act_step)
            for t in range(LT):
                link(act.activation(square[:, :], branch[:, t, :], ACT.Square, accum_out=ss[:, t:t + 1]))
            act.activation(rstd[:, :], ss[:, :], ACT.Sqrt, scale=1.0 / D, bias=k.const("eps")).then_inc(root_ready, 1)

        @block.vector
        def _(dve):
            link = Steps(dve, step)
            dve.wait_ge(root_ready, 1)
            link(dve.reciprocal(rstd[:, :], rstd[:, :]))
            for t in range(LT):
                link(dve.scalar_tensor_tensor(branch[:, t, :], branch[:, t, :], rstd[:, t:t + 1], gain_rows, ALU.mult, ALU.mult))
                link(dve.tensor_tensor(x[:, t, :], x[:, t, :], branch[:, t, :], ALU.add))


def first_mixer(k, x_in, x_out, dump=None):
    nc = k.nc
    vec, taps, mod, scales, gains, gnorm = k.first
    w_in = k.dram["w_in"][0]
    dump = dump or (lambda name, ap: None)
    column_vectors(k, "vec_a", [k.dram["b_ada"][0].rearrange("(n p) -> n p", p=P)]
                   + [k.dram[n][0].rearrange("(n p) -> n p", p=P) for n in ("norm_pre_mix", "norm_post_mix", "norm_pre_ffn", "norm_post_ffn")]
                   + [k.dram["c"][0].rearrange("(n p) -> n p", p=P), k.dram["c_ctx"].rearrange("(n p) -> n p", p=P),
                      k.dram["ssd_conv_b"][0].rearrange("(n p) -> n p", p=P)], vec)
    column_vectors(k, "vec_b", [k.dram["ssd_conv_w"][0].rearrange("k (n p) -> (k n) p", p=P)], taps)
    column_vectors(k, "vec_n", [k.dram["ssd_norm"][0].rearrange("(n p) -> n p", p=P)], gnorm)
    modulations(k, vec, mod, scales, gains)
    dump("mod", mod)

    def tile(scope, name, shape):
        return scope.enter_context(nc.sbuf_tensor(name, shape, F32))

    def context_cols(label, hcT):
        with ExitStack() as s:
            rows = tile(s, label + "_rows", [P, CT_TILES, D])
            load(k, label + "_load", [(rows[:, :, :], rows_view(k.dram["ctx"]))])
            norm_transpose(k, label, rows, CT_TILES, hcT, scales[:, KD:2 * KD], mod[:, SH1:SH1 + KD, 1])

    with ExitStack() as outer:
        uT = tile(outer, "uT", [P, KD, L])
        with ExitStack() as mid:
            hT = tile(mid, "hT", [P, KD, L])
            with ExitStack() as s:
                rows = tile(s, "x_rows", [P, LT, D])
                load(k, "x_load", [(rows[:, :, :], rows_view(x_in))])
                norm_transpose(k, "x_norm", rows, LT, hT, scales[:, 0:KD], mod[:, SH1:SH1 + KD, 0])
            dump("hT", hT)

            def cols_of(xT, n, place):
                return lambda wt, c: [(lambda j, m=m: wt[:, j, m * P:(m + 1) * P], lambda j: xT[:, j, :], P, n, at(place, 4 * c + m))
                                      for m in range(4)]

            with ExitStack() as s:
                load_constants(k, s, "na")
                kc, vc = tile(s, "kc", [P, KD, CTX]), tile(s, "vc", [P, CT_TILES, D])
                q, key, v = tile(s, "q", [P, KD, L]), tile(s, "key", [P, KD, L]), tile(s, "v", [P, LT, D])
                w_q, w_k, w_v = (w_in[:, a:a + D] for a in (COL_Q, COL_K, COL_V))
                with ExitStack() as s2:
                    hcT = tile(s2, "hcT_na", [P, KD, CTX])
                    ahead = WeightsAhead(k, s2, "ahead_qkv")
                    ahead.start(w_k, KD, 512)
                    context_cols("ctx_na", hcT)
                    project(k, "p_kc", w_k, KD, 512, 2, cols_of(hcT, CTX, kc), ahead=ahead, then=(w_v, KD, 512))
                    project(k, "p_vc", w_v, KD, 512, 2,
                            lambda wt, c: [(lambda j, t=t: hcT[:, j, t * P:(t + 1) * P], lambda j: wt[:, j, :], P, 512,
                                            vc[:, t, bass.ds(c * 512, 512)]) for t in range(CT_TILES)], ahead=ahead, then=(w_q, KD, 512))
                    project(k, "p_q", w_q, KD, 512, 2, cols_of(hT, L, q), ahead=ahead, then=(w_k, KD, 512))
                    project(k, "p_k", w_k, KD, 512, 2, cols_of(hT, L, key), ahead=ahead, then=(w_v, KD, 512))
                    project_rows(k, "p_v", w_v, KD, hT, v, 2, ahead=ahead)
                o = tile(s, "o_na", [P, LT, D])
                rotate(k, q, key)
                neighbourhood_attention(k, q, key, kc, v, vc, o)
                dump("o_na", o)
                oT = q
                w_gate = w_in[:, COL_GNA:COL_GNA + D]
                ahead = WeightsAhead(k, s, "ahead_na")
                ahead.start(w_gate, KD, 512)
                transpose_rows(k, "o_na_t", o, LT, KD, oT)
                gated_branch(k, "na_br", w_gate, hT, k.dram["w_branch_na"][0], KD, oT, uT, add=False, ahead=ahead)

            with ExitStack() as s:
                xs = tile(s, "xs", [P, LT, SSD_W])
                y = tile(s, "y", [P, LT, SSD_W])
                with ExitStack() as s1:
                    dt, a = tile(s1, "dt", [P, N_SEG, 64]), tile(s1, "a", [P, N_SEG, 64])
                    dec = tile(s1, "dec", [P, 2 * N_SEG, 96])
                    bcT = tile(s1, "bcT", [P, 2 * SSD_G, L])
                    b_rows, bc_rows = tile(s1, "b_rows", [P, LT, 512]), tile(s1, "bc_rows", [P, CT_TILES, 512])
                    xsc = tile(s1, "xsc", [P, CT_TILES, SSD_W])
                    with ExitStack() as s2:
                        hcT = tile(s2, "hcT_ssd", [P, KD, CTX])
                        context_cols("ctx_ssd", hcT)
                        ahead = WeightsAhead(k, s2, "ahead_conv")
                        ahead.start(w_in[:, COL_XBC + 16 * P:COL_XBC + XBC], KD, 256)
                        ssd_steps(k, hT, hcT, dt, a, dec)
                        xw = y[:, 0:2, :].rearrange("p a (b n) -> p (a b) n", n=L)
                        xcw = y[:, 2, :].rearrange("p (b n) -> p b n", n=CTX)
                        pads = (y[:, 3, 0:L + 4], y[:, 3, 520:520 + CTX + 4], y[:, 3, 1024:1024 + L])
                        clear(k, "pads", [y[:, 3, :]])
                        conv_silu(k, "conv_bc", hT, hcT, pads, 16, 4, vec, taps, bcT[:, 0:4, :], xcw,
                                  [(j, b_rows, bc_rows, j * P) for j in range(4)], ahead, 20)
                        conv_silu(k, "conv_c", hT, hcT, pads, 20, 4, vec, taps, bcT[:, 4:8, :], xcw, [], ahead, 0)
                        for part in range(2):
                            conv_silu(k, f"conv_x{part}", hT, hcT, pads, 8 * part, 8, vec, taps, xw, xcw,
                                      [(j, xs, xsc, (8 * part + j) * P) for j in range(8)], ahead, None if part else 8)
                    dump("xs", xs); dump("bcT", bcT); dump("dt", dt)
                    ssd_scan(k, xs, xsc, bcT[:, 0:4, :], bcT[:, 4:8, :], b_rows, bc_rows, dt, a, dec, y)
                dump("y", y)
                ahead = WeightsAhead(k, s, "ahead_ssd")
                w_z, w_gate = w_in[:, COL_Z:COL_Z + SSD_W], w_in[:, COL_GSSD:COL_GSSD + D]
                ahead.start(w_z, KD, 512)
                with ExitStack() as s1:
                    z = tile(s1, "z", [P, LT, SSD_W])
                    skip = tile(s1, "skip", [P, SSD_H])
                    load(k, "skip_load", [(skip[:, :], k.dram["ssd_d_skip"][0:1, :].to_broadcast([P, SSD_H]))])
                    project(k, "p_z", w_z, KD, 512, 4,
                            lambda wt, c: [(lambda j, t=t: hT[:, j, t * P:(t + 1) * P], lambda j: wt[:, j, :], P, 512,
                                            z[:, t, bass.ds(c * 512, 512)]) for t in range(LT)],
                            lambda act, link, product, place, c, g, extra: act.activation(place, product, ACT.Silu), engine="scalar",
                            ahead=ahead, then=(w_gate, KD, 512))
                    ssd_gate_norm(k, y, xs, z, skip)
                yT = xs[:, :, :].rearrange("p a (b n) -> p (a b) n", n=L)
                transpose_rows(k, "y_t", y, LT, SSD_W // P, yT, gnorm)
                gated_branch(k, "ssd_br", w_gate, hT, k.dram["w_branch_ssd"][0], SSD_W // P, yT, uT, add=True, ahead=ahead,
                             then=(k.dram["w_out"][0], KD, 512))
                dump("uT", uT)
                x, mix, gain_rows = tile(s, "x1", [P, LT, D]), tile(s, "mix", [P, LT, D]), tile(s, "gain1", [P, D])
                load(k, "x1_load", [(x[:, :, :], rows_view(x_in))])
                spread_columns(k, "gain1s", gains[:, 0, :], gain_rows[:, :])
                project_rows(k, "p_out", k.dram["w_out"][0], KD, uT, mix, 2, ahead=ahead)
                add_normed(k, "add1", x, mix, gain_rows[:, :])
                load(k, "x1_store", [(rows_view(x_out), x[:, :, :])])


def clear(k, label, tiles):
    ctx, sb, ps, sem = stage(k, label)
    with ctx:
        done = sem("done")
        block = ctx.enter_context(k.nc.Block())

        @block.vector
        def _(dve):
            for t in tiles:
                dve.memset(t, 0.0).then_inc(done, 1)
            dve.wait_ge(done, len(tiles))


SLOTS = 64


def expert_weights(w, e):
    return w[0][bass.ds(e, 1)].rearrange("a d f -> (a d) f")


def run_experts(k, label, n_e, ff, load_gate_up, down_w, xn, rank, gate, scale_cols, shift_cols, out):
    nc = k.nc
    ctx, sb, ps, sem = stage(k, label)
    SET = 2 * P
    NS = ff // SET
    PER = KD // NS
    pairs = n_e // 2
    M = 2 * NS
    PIECES = 2 * LT + 1
    with ctx:
        wgu = sb("wgu", [P, 2, 2, KD, 2, SET])
        wd = sb("wd", [P, 2, 2, 2, D])
        places = sb("places", [P, LT, n_e + 2])
        sel, gated = sb("sel", [P, LT, 2 * SLOTS]), sb("gated", [P, LT, 2 * SLOTS])
        selT, y = sb("selT", [P, L]), sb("y", [P, D])
        xg = sb("xg", [P, 2, KD, 2 * SLOTS])
        silu, hid, hidT = sb("silu", [P, 2, SET]), sb("hid", [P, 2, SET]), sb("hidT", [P, 2, SET])
        gu, turn, acc, grp, piece = ps("gu", [P, 2, 512]), ps("turn", [P, 2, SET]), ps("acc", [P, 2, 512]), ps("grp", [P, 4, P]), ps("piece", [P, 2, 512])
        gu_loaded, d_loaded = [sem("gu_loaded0"), sem("gu_loaded1")], [sem("d_loaded0"), sem("d_loaded1")]
        gu_done, silu_ready, hid_ready, turned, hidT_ready, down_done, y_ready = (
            sem(x) for x in ("gu_done", "silu_ready", "hid_ready", "turned", "hidT_ready", "down_done", "y_ready"))
        places_ready, sel_ready, gated_ready, gathered, xg_ready, piece_done, piece_taken = (
            sem(x) for x in ("places_ready", "sel_ready", "gated_ready", "gathered", "xg_ready", "piece_done", "piece_taken"))
        block = ctx.enter_context(nc.Block())

        @block.sync
        def _(sp):
            with sp.Fori(0, pairs // 2) as i:
                for m in range(M):
                    u, s, b = m // NS, m % NS, m % 2
                    sp.wait_ge(gu_done, i * M + (m + 1))
                    for e in range(2):
                        for dst, src in load_gate_up(4 * i + (2 * u + e), s, wgu[:, b, e]):
                            sp.dma_start(dst, src).then_inc(gu_loaded[b], 16)
                    sp.wait_ge(down_done, i * M + (m + 1))
                    for e in range(2):
                        sp.dma_start(wd[:, b, e], down_w(4 * i + (2 * u + e), s).rearrange("(k p) n -> p k n", p=P)).then_inc(d_loaded[b], 16)

        def next_tokens(s):
            js = list(range(s * PER, (s + 1) * PER))
            return (js[:PER // 2], js[PER // 2:]) if PER > 1 else ([], js)

        n_loads = 2 * len(load_gate_up(0, 0, wgu[:, 0, 0]))

        @block.tensor
        def _(pe):
            def gather(js):
                for j in js:
                    for t in range(LT):
                        last = pe.matmul(grp[:, j % 4, :], xn[:, t, j * P:(j + 1) * P], sel[:, t, :], start=(t == 0), stop=(t == LT - 1))
                last.then_inc(gathered, len(js))

            def scatter(n, slot, free):
                pe.wait_ge(piece_taken, free)
                t, h = n // 2, n % 2
                pe.matmul(piece[:, slot, :], selT[:, t * P:(t + 1) * P], y[:, h * 512:(h + 1) * 512], start=True,
                          stop=True).then_inc(piece_done, 1)

            pe.sem_inc(gu_done, 2)
            pe.sem_inc(down_done, 2)
            pe.sem_inc(turned, 2)
            pe.wait_ge(sel_ready, 1)
            gather(range(4))
            pe.wait_ge(xg_ready, 4)
            gather(range(4, KD))
            with pe.Fori(0, pairs // 2) as i:
                for m in range(M):
                    u, s, b = m // NS, m % NS, m % 2
                    if s == 0:
                        pe.wait_ge(xg_ready, i * (2 * KD) + KD * (u + 1))
                    pe.wait_ge(gu_loaded[b], i * (16 * n_loads * NS) + 16 * n_loads * (m // 2 + 1))
                    pe.wait_ge(hid_ready, i * M + (m + 1))
                    for j in range(KD):
                        for e in range(2):
                            half = slice(e * SLOTS, (e + 1) * SLOTS)
                            last = pe.matmul(gu[half, b, :], xg[:, u, j, half], wgu[:, b, e, j].rearrange("p a n -> p (a n)"),
                                             start=(j == 0), stop=(j == KD - 1))
                    last.then_inc(gu_done, 1)
                    before, after = next_tokens(s)
                    pe.wait_ge(sel_ready, 2 * i + (u + 2))
                    if before:
                        pe.wait_ge(xg_ready, i * (2 * KD) + (KD * (u + 1) + before[0]))
                        gather(before)
                    pe.wait_ge(y_ready, 2 * i + (u + 1))
                    pe.wait_ge(piece_taken, i * (2 * PIECES) + (PIECES * u + 2))
                    for n in range(s * PER, (s + 1) * PER):
                        scatter(n, (PIECES * u + n) % 2, i * (2 * PIECES) + (PIECES * u + n + 1))
                    if s == NS - 1:
                        n = 2 * LT
                        pe.wait_ge(gated_ready, 2 * i + (u + 1))
                        pe.wait_ge(piece_taken, i * (2 * PIECES) + (PIECES * u + n + 1))
                        for t in range(LT):
                            last = pe.transpose(piece[:, (PIECES * u + n) % 2, t * P:(t + 1) * P], gated[:, t, :], k.const("ident"))
                        last.then_inc(piece_done, 1)
                    pe.wait_ge(hid_ready, i * M + (m + 3))
                    pe.wait_ge(hidT_ready, i * M + (m + 1))
                    for f in range(2):
                        last = pe.transpose(turn[:, b, f * P:(f + 1) * P], hid[:, b, f * P:(f + 1) * P], k.const("ident"))
                    last.then_inc(turned, 1)
                    pe.wait_ge(xg_ready, i * (2 * KD) + (KD * (u + 1) + after[0]))
                    gather(after)
                    pe.wait_ge(d_loaded[b], i * (32 * NS) + 32 * (m // 2 + 1))
                    pe.wait_ge(hidT_ready, i * M + (m + 3))
                    for f in range(2):
                        for h in range(2):
                            for e in range(2):
                                half = slice(e * SLOTS, (e + 1) * SLOTS)
                                last = pe.matmul(acc[half, h, :], hidT[:, b, f * P + e * SLOTS:f * P + (e + 1) * SLOTS],
                                                 wd[:, b, e, f, h * 512:(h + 1) * 512], start=(s == 0 and f == 0), stop=(s == NS - 1 and f == 1))
                    last.then_inc(down_done, 1)
            pe.wait_ge(y_ready, pairs + 1)
            pe.wait_ge(piece_taken, pairs * PIECES + 2)
            for n in range(2 * LT):
                scatter(n, n % 2, pairs * PIECES + n + 1)

        @block.scalar
        def _(act):
            act.preload_act_table(ACT.Silu)
            act.sem_inc(hidT_ready, 2)
            with act.Fori(0, pairs // 2) as i:
                for m in range(M):
                    u, s, b = m // NS, m % NS, m % 2
                    act.wait_ge(gu_done, i * M + (m + 3))
                    act.wait_ge(hid_ready, i * M + (m + 1))
                    act.activation(silu[:, b, :], gu[:, b, 0:SET], ACT.Silu).then_inc(silu_ready, 1)
                    act.wait_ge(turned, i * M + (m + 3))
                    act.wait_ge(down_done, i * M + (m + 1))
                    act.activation(hidT[:, b, :], turn[:, b, :], ACT.Copy).then_inc(hidT_ready, 1)
                    if s == NS - 1:
                        act.wait_ge(down_done, i * M + (m + 3))
                        act.activation(y[:, :], acc[:, :, :].rearrange("p b n -> p (b n)"), ACT.Copy).then_inc(y_ready, 1)

        @block.vector
        def _(dve):
            def one_hots(p, e):
                return dve.tensor_tensor(sel[:, :, e * SLOTS:(e + 1) * SLOTS], k.const("slots").unsqueeze(1).to_broadcast([P, LT, SLOTS]),
                                         places[:, :, bass.ds(2 * p + e, 1)].to_broadcast([P, LT, SLOTS]), ALU.is_equal)

            def gathered_tokens(js, buffer, count):
                dve.wait_ge(gathered, count)
                for j in js:
                    if shift_cols is None:
                        ins = dve.tensor_scalar(xg[:, buffer, j, :], grp[:, j % 4, :], scale_cols[:, j:j + 1], None, ALU.mult)
                    else:
                        ins = dve.tensor_scalar(xg[:, buffer, j, :], grp[:, j % 4, :], scale_cols[:, j:j + 1], shift_cols[:, j:j + 1], ALU.mult, ALU.add)
                    ins.then_inc(xg_ready, 1)

            def add_scattered(n, slot, count):
                dve.wait_ge(piece_done, count)
                place = out[:, n // 2, (n % 2) * 512:(n % 2 + 1) * 512]
                dve.tensor_tensor(place, place, piece[:, slot, :], ALU.add).then_inc(piece_taken, 1)

            dve.memset(places[:, :, n_e:n_e + 2], 0.0).then_inc(places_ready, 1)
            dve.tensor_copy(places[:, :, 0:n_e], rank[:, :, :]).then_inc(places_ready, 1)
            dve.memset(y[:, :], 0.0).then_inc(y_ready, 1)
            dve.memset(selT[:, :], 0.0).then_inc(piece_taken, 2)
            dve.sem_inc(hid_ready, 2)
            dve.wait_ge(places_ready, 2)
            one_hots(0, 0).then_inc(places_ready, 1)
            one_hots(0, 1).then_inc(sel_ready, 1)
            gathered_tokens(range(4), 0, 4)
            gathered_tokens(range(4, KD), 0, KD)
            dve.wait_ge(places_ready, 3)
            with dve.Fori(0, pairs // 2) as i:
                for m in range(M):
                    u, s, b = m // NS, m % NS, m % 2
                    if s == 0:
                        dve.wait_ge(sel_ready, 2 * i + (u + 1))
                        if u:
                            dve.wait_ge(piece_taken, i * (2 * PIECES) + (PIECES * u + 2))
                        for e in range(2):
                            half = slice(e * SLOTS, (e + 1) * SLOTS)
                            ins = dve.tensor_tensor(gated[:, :, half], sel[:, :, half],
                                                    gate[:, :, bass.ds(4 * i + (2 * u + e), 1)].to_broadcast([P, LT, SLOTS]), ALU.mult)
                            ins.then_inc(gated_ready if e else places_ready, 1)
                        dve.wait_ge(gated_ready, 2 * i + (u + 1))
                        dve.wait_ge(places_ready, i * 4 + (2 * u + 4))
                        one_hots(2 * i + (u + 1), 0).then_inc(places_ready, 1)
                        one_hots(2 * i + (u + 1), 1).then_inc(sel_ready, 1)
                        dve.wait_ge(places_ready, i * 4 + (2 * u + 5))
                    dve.wait_ge(silu_ready, i * M + (m + 1))
                    dve.wait_ge(turned, i * M + (m + 1))
                    dve.tensor_tensor(hid[:, b, :], silu[:, b, :], gu[:, b, SET:2 * SET], ALU.mult).then_inc(hid_ready, 1)
                    before, after = next_tokens(s)
                    if before:
                        gathered_tokens(before, 1 - u, i * (2 * KD) + (KD * (u + 1) + before[-1] + 1))
                    for n in range(s * PER, (s + 1) * PER):
                        add_scattered(n, (PIECES * u + n) % 2, i * (2 * PIECES) + (PIECES * u + n + 1))
                    if s == NS - 1:
                        n = 2 * LT
                        dve.wait_ge(piece_done, i * (2 * PIECES) + (PIECES * u + n + 1))
                        dve.tensor_copy(selT[:, :], piece[:, (PIECES * u + n) % 2, :]).then_inc(piece_taken, 1)
                    gathered_tokens(after, 1 - u, i * (2 * KD) + (KD * (u + 1) + after[-1] + 1))
            for n in range(2 * LT):
                add_scattered(n, n % 2, pairs * PIECES + n + 1)
            dve.wait_ge(piece_taken, pairs * PIECES + 2 * LT + 2)


def choose_tokens(k, h2T, w_router, rank, aff):
    nc = k.nc
    ctx, sb, ps, sem = stage(k, "choose")
    E = EC_E
    with ctx:
        w = sb("w", [P, KD, E])
        top, total = sb("top", [P, LT]), sb("total", [P, LT])
        affT, left, chosenT, eight = sb("affT", [E, L]), sb("left", [E, L]), sb("chosenT", [E, L]), sb("eight", [E, 8])
        chosen = sb("chosen", [P, LT, E])
        score, wide, count = ps("score", [P, 512]), ps("wide", [P, 512]), ps("count", [P, 512])
        loaded, scored, exp_in, exp_out, aff_ready, wide_ready, chosen_T, back, chosen_ready, counted, step = (
            sem(x) for x in ("loaded", "scored", "exp_in", "exp_out", "aff_ready", "wide_ready", "chosen_T", "back", "chosen_ready", "counted", "step"))
        block = ctx.enter_context(nc.Block())

        @block.sync
        def _(sp):
            sp.dma_start(w[:, :, :], w_router.rearrange("(k p) n -> p k n", p=P)).then_inc(loaded, 16)

        @block.tensor
        def _(pe):
            pe.wait_ge(loaded, 16)
            for t in range(LT):
                for j in range(KD):
                    last = pe.matmul(score[:, t * E:(t + 1) * E], h2T[:, j, t * P:(t + 1) * P], w[:, j, :], start=(j == 0), stop=(j == KD - 1))
            last.then_inc(scored, 1)
            pe.wait_ge(aff_ready, 1)
            for t in range(LT):
                last = pe.transpose(wide[0:E, t * P:(t + 1) * P], aff[:, t, :], k.const("ident"))
            last.then_inc(wide_ready, 1)
            pe.wait_ge(chosen_T, 1)
            for t in range(LT):
                last = pe.transpose(score[:, t * E:(t + 1) * E], chosenT[:, t * P:(t + 1) * P], k.const("ident", E)[:, 0:E])
            last.then_inc(back, 1)
            pe.wait_ge(chosen_ready, 1)
            for t in range(LT):
                for u in range(t + 1):
                    last = pe.matmul(count[:, t * E:(t + 1) * E], k.const("upto" if u == t else "ones"), chosen[:, u, :],
                                     start=(u == 0), stop=(u == t))
            last.then_inc(counted, 1)

        @block.scalar
        def _(act):
            act.wait_ge(exp_in, 1)
            act.activation(aff[:, :, :], aff[:, :, :], ACT.Exp).then_inc(exp_out, 1)

        @block.vector
        def _(dve):
            link = Steps(dve, step)
            dve.wait_ge(scored, 1)
            s = score[:, 0:LT * E].rearrange("p (t e) -> p t e", e=E)
            link(dve.tensor_reduce(top[:, :], s, AX.X, ALU.max))
            dve.tensor_tensor(aff[:, :, :], s, top[:, :].unsqueeze(2).to_broadcast([P, LT, E]), ALU.subtract).then_inc(exp_in, 1)
            dve.wait_ge(exp_out, 1)
            link(dve.tensor_reduce(total[:, :], aff[:, :, :], AX.X, ALU.add))
            link(dve.reciprocal(total[:, :], total[:, :]))
            dve.tensor_tensor(aff[:, :, :], aff[:, :, :], total[:, :].unsqueeze(2).to_broadcast([P, LT, E]), ALU.mult).then_inc(aff_ready, 1)
            dve.wait_ge(wide_ready, 1)
            link(dve.tensor_copy(affT[:, :], wide[0:E, :]))
            link(dve.tensor_copy(left[:, :], affT[:, :]))
            for _ in range(EC_CAP // 8):
                link(dve.max(eight[:, :], left[:, :]))
                link(dve.match_replace(left[:, :], eight[:, :], left[:, :], -1.0))
            dve.tensor_tensor(chosenT[:, :], left[:, :], affT[:, :], ALU.not_equal).then_inc(chosen_T, 1)
            dve.wait_ge(back, 1)
            dve.tensor_copy(chosen[:, :, :].rearrange("p t e -> p (t e)"), score[:, 0:LT * E]).then_inc(chosen_ready, 1)
            dve.wait_ge(counted, 1)
            dve.wait_ge(chosen_ready, 1)
            link(dve.tensor_tensor(rank[:, :, :].rearrange("p t e -> p (t e)"), count[:, 0:LT * E],
                                   chosen[:, :, :].rearrange("p t e -> p (t e)"), ALU.mult))


def first_experts(k, x_in, x_out, dump=None):
    nc = k.nc
    vec, taps, mod, scales, gains, gnorm = k.first
    dump = dump or (lambda name, ap: None)

    def tile(scope, name, shape):
        return scope.enter_context(nc.sbuf_tensor(name, shape, F32))

    with ExitStack() as outer:
        out = tile(outer, "ec_out", [P, LT, D])
        clear(k, "ec_clear", [out[:, :, :]])
        with ExitStack() as s:
            xn, rank, aff = tile(s, "ec_xn", [P, LT, D]), tile(s, "ec_rank", [P, LT, EC_E]), tile(s, "ec_aff", [P, LT, EC_E])
            sc, sh = scales[:, 2 * KD:3 * KD], mod[:, SH2:SH2 + KD, 0]
            with ExitStack() as s1:
                rows, h2T = tile(s1, "ec_rows", [P, LT, D]), tile(s1, "ec_h2T", [P, KD, L])
                load(k, "ec_load", [(rows[:, :, :], rows_view(x_in))])
                norm_transpose(k, "ec_norm", rows, LT, h2T, sc, sh, xn=xn)
                choose_tokens(k, h2T, k.dram["w_router"][0], rank, aff)
                dump("ec_rank", rank)

            def gate_up(e, s, dst):
                return [(dst[:, :, half, :], expert_weights(k.dram[name], e)[:, s * 256:(s + 1) * 256].rearrange("(k p) n -> p k n", p=P))
                        for half, name in enumerate(("w_exp_gate", "w_exp_up"))]

            run_experts(k, "ec", EC_E, EC_FF, gate_up, lambda e, s: expert_weights(k.dram["w_exp_down"], e)[s * 256:(s + 1) * 256, :],
                        xn, rank, aff, sc, sh, out)
        dump("ec_out", out)
        x, gain_rows = tile(outer, "x2", [P, LT, D]), tile(outer, "gain2", [P, D])
        load(k, "x2_load", [(x[:, :, :], rows_view(x_in))])
        spread_columns(k, "gain2s", gains[:, 1, :], gain_rows[:, :])
        add_normed(k, "add2", x, out, gain_rows[:, :])
        load(k, "x2_store", [(rows_view(x_out), x[:, :, :])])


W2_MIX, W2_FFN, W2_QA, W2_KVA, W2_MU = 0, 8, 16, 19, 21
RW_CH = L // RW_C
RW_PAIRS = RW_H // 2


def rw_lora(k, hT, mu_cols, lw, a, g):
    nc = k.nc
    ctx, sb, ps, sem = stage(k, "lora")
    c0 = 3 * RW_D
    with ctx:
        w = sb("w", [P, KD, 256])
        up = sb("up", [P, RW_D])
        g_up = sb("g_up", [P, RW_D])
        w0, a0 = sb("w0", [P, RW_D]), sb("a0", [P, RW_D])
        late = sb("late", [P, 2, L + 1])
        step_back = sb("step_back", [P, 2, L])
        z = sb("z", [P, 2, L])
        down = ps("down", [P, 2, 512])
        prod = ps("prod", [P, 3, 512])
        loaded, ready, mixed, squashed, up_ready, up_taken, pre, done, step = (
            sem(x) for x in ("loaded", "ready", "mixed", "squashed", "up_ready", "up_taken", "pre", "done", "step"))
        block = ctx.enter_context(nc.Block())
        dr = k.dram

        @block.sync
        def _(sp):
            sp.dma_start(w[:, :, :], dr["w_in_2"][0][:, c0:c0 + 256].rearrange("(k p) n -> p k n", p=P)).then_inc(loaded, 16)
            sp.dma_start(up[0:64, :], dr["rw_w_up_2"][0]).then_inc(loaded, 16)
            sp.dma_start(up[64:128, :], dr["rw_a_up_2"][0]).then_inc(loaded, 16)
            sp.dma_start(g_up[:, :], dr["rw_g_up_2"][0]).then_inc(loaded, 16)
            sp.dma_start(w0[:, :], dr["rw_w0_2"][0:1, :].to_broadcast([P, RW_D])).then_inc(loaded, 16)
            sp.dma_start(a0[:, :], dr["rw_a0_2"][0:1, :].to_broadcast([P, RW_D])).then_inc(loaded, 16)

        @block.tensor
        def _(pe):
            pe.wait_ge(loaded, 16 * 6)
            for m in range(2):
                for j in range(KD):
                    last = pe.matmul(down[:, m, :], w[:, j, m * P:(m + 1) * P], hT[:, j, :], start=(j == 0), stop=(j == KD - 1))
            last.then_inc(ready, 1)
            pe.wait_ge(squashed, 2)
            for t in range(LT):
                rows = slice(t * P, (t + 1) * P)
                for n, (z_t, u) in enumerate(((z[0:64, 0, rows], up[0:64, :]), (z[64:128, 0, rows], up[64:128, :]), (z[:, 1, rows], g_up[:, :]))):
                    if t:
                        pe.wait_ge(up_taken, 3 * (t - 1) + n + 1)
                    pe.matmul(prod[:, n, :], z_t, u, start=True, stop=True).then_inc(up_ready, 1)

        @block.vector
        def _(dve):
            link = Steps(dve, step)
            link(dve.memset(late[:, :, 0:1], 0.0))
            dve.wait_ge(ready, 1)
            for m in range(2):
                link(dve.tensor_copy(late[:, m, 1:L + 1], down[:, m, :]))
                link(dve.tensor_tensor(step_back[:, m, :], late[:, m, 0:L], late[:, m, 1:L + 1], ALU.subtract))
                dve.scalar_tensor_tensor(z[:, m, :], step_back[:, m, :], mu_cols[:, m:m + 1], late[:, m, 1:L + 1],
                                         ALU.mult, ALU.add).then_inc(mixed, 1)
            for t in range(LT):
                for n, (dst, bias) in enumerate(((lw, w0), (a, a0), (g, None))):
                    dve.wait_ge(up_ready, 3 * t + n + 1)
                    if bias is None:
                        dve.tensor_copy(dst[:, t, :], prod[:, n, :]).then_inc(up_taken, 1)
                    else:
                        dve.tensor_tensor(dst[:, t, :], prod[:, n, :], bias[:, :], ALU.add).then_inc(up_taken, 1)
            dve.wait_ge(done, 2)
            link(dve.tensor_scalar(lw[:, :, :], lw[:, :, :], -float(np.exp(-0.5)), None, ALU.mult))

        @block.scalar
        def _(act):
            act.wait_ge(mixed, 2)
            act.activation(z[0:64, 0, :], z[0:64, 0, :], ACT.Tanh).then_inc(squashed, 1)
            act.activation(z[:, 1, :], z[:, 1, :], ACT.Sigmoid).then_inc(squashed, 1)
            act.wait_ge(up_taken, 3 * LT)
            act.activation(lw[:, :, :], lw[:, :, :], ACT.Sigmoid).then_inc(done, 1)
            act.activation(a[:, :, :], a[:, :, :], ACT.Sigmoid).then_inc(done, 1)


def rw_shift(k, z):
    nc = k.nc
    n = 3 * RW_D
    ctx, sb, ps, sem = stage(k, "shift")
    with ctx:
        mu, late = sb("mu", [P, n]), sb("late", [P, LT, n])
        cleared, loaded, shifted, late_ready, step = (sem(x) for x in ("cleared", "loaded", "shifted", "late_ready", "step"))
        block = ctx.enter_context(nc.Block())

        @block.sync
        def _(sp):
            sp.dma_start(mu[:, :], k.dram["rw_mu_2"][0:1, 0:n].to_broadcast([P, n])).then_inc(loaded, 16)
            sp.dma_start(late[1:P, :, :], z[0:P - 1, :, :]).then_inc(loaded, 16)
            sp.dma_start(late[0:1, 1:LT, :], z[P - 1:P, 0:LT - 1, :]).then_inc(loaded, 16)
            sp.wait_ge(cleared, 1)

        @block.vector
        def _(dve):
            link = Steps(dve, step)
            dve.memset(late[0:1, 0, :], 0.0).then_inc(cleared, 1)
            dve.wait_ge(loaded, 48)
            dve.wait_ge(cleared, 1)
            for t in range(LT):
                link(dve.tensor_tensor(late[:, t, :], late[:, t, :], z[:, t, :], ALU.subtract))
                link(dve.tensor_tensor(late[:, t, :], late[:, t, :], mu[:, :], ALU.mult))
                link(dve.tensor_tensor(z[:, t, :], z[:, t, :], late[:, t, :], ALU.add))


def rw_scaled(k, z, lw, a, Q, R, K, B, D_next, bonus):
    nc = k.nc
    ctx, sb, ps, sem = stage(k, "scaled")
    S3 = [P, LT, RW_H, 64]
    with ctx:
        k_k, k_a, r_k = sb("k_k", [P, RW_D]), sb("k_a", [P, RW_D]), sb("r_k", [P, RW_D])
        work = sb("work", [P, LT, RW_D])
        ss = sb("ss", [P, LT, RW_H])
        inv = sb("inv", [P, LT, RW_D])
        now = ps("now", [P, LT, 512])
        ends = ps("ends", [P, 512])
        dsum = sb("dsum", [P, RW_PAIRS, 2 * RW_CH])
        loaded, cum_ready, cum_taken, ss_ready, root_ready, now_ready, before_ready, inv_ready, ends_ready, d_ready, step = (
            sem(x) for x in ("loaded", "cum_ready", "cum_taken", "ss_ready", "root_ready", "now_ready", "before_ready", "inv_ready", "ends_ready", "d_ready", "step"))
        block = ctx.enter_context(nc.Block())
        r, key = z[:, :, 0:RW_D], z[:, :, RW_D:2 * RW_D]

        def heads(t):
            return t.rearrange("p t (h d) -> p t h d", d=64)

        def rows(t):
            return t[:, :].unsqueeze(1).to_broadcast([P, LT, RW_D])

        @block.sync
        def _(sp):
            for dst, name in ((k_k, "rw_k_k_2"), (k_a, "rw_k_a_2")):
                sp.dma_start(dst[:, :], k.dram[name][0:1, :].to_broadcast([P, RW_D])).then_inc(loaded, 16)
            sp.dma_start(r_k[:, :], k.dram["rw_r_k_2"].rearrange("a h d -> a (h d)").to_broadcast([P, RW_D])).then_inc(loaded, 16)

        @block.tensor
        def _(pe):
            for t in range(LT):
                last = pe.matmul(now[:, t, :], k.const("rw_mid"), lw[:, t, :], start=True, stop=True)
            last.then_inc(cum_ready, 1)
            for p in range(RW_PAIRS):
                for t in range(LT):
                    last = pe.matmul(ends[:, p * 16 + 4 * t:p * 16 + 4 * t + 4], lw[:, t, p * P:(p + 1) * P], k.const("rw_dlo"),
                                     start=True, stop=True)
            last.then_inc(ends_ready, 1)
            pe.wait_ge(now_ready, 2)
            for t in range(LT):
                last = pe.matmul(now[:, t, :], k.const("rw_midx"), lw[:, t, :], start=True, stop=True)
            last.then_inc(cum_ready, 1)

        @block.scalar
        def _(act):
            act.wait_ge(cum_ready, 1)
            act.activation(R[:, :, :], now[:, :, :], ACT.Exp).then_inc(now_ready, 1)
            act.activation(inv[:, :, :], now[:, :, :], ACT.Exp, scale=-1.0).then_inc(now_ready, 1)
            act.wait_ge(cum_ready, 2)
            act.activation(Q[:, :, :], now[:, :, :], ACT.Exp).then_inc(before_ready, 1)
            act.wait_ge(d_ready, 1)
            act.activation(D_next[:, :, 0:RW_CH - 1], D_next[:, :, 0:RW_CH - 1], ACT.Exp).then_inc(d_ready, 1)
            act.wait_ge(ss_ready, 1)
            act.activation(ss[:, :, :], ss[:, :, :], ACT.Sqrt).then_inc(root_ready, 1)

        @block.vector
        def _(dve):
            link = Steps(dve, step)
            dve.wait_ge(ends_ready, 1)
            link(dve.tensor_copy(dsum[:, :, :], ends[:, 0:RW_PAIRS * 16].rearrange("p (a c) -> p a c", c=16)))
            dve.tensor_tensor(D_next[:, :, 0:RW_CH - 1], dsum[:, :, 1:2 * RW_CH - 1:2], dsum[:, :, 2:2 * RW_CH:2], ALU.add).then_inc(d_ready, 1)
            dve.wait_ge(loaded, 48)
            link(dve.tensor_tensor(B[:, :, :], key, rows(k_k), ALU.mult))
            link(dve.tensor_tensor(work[:, :, :], B[:, :, :], B[:, :, :], ALU.mult))
            dve.tensor_reduce(ss[:, :, :], heads(work[:, :, :]), AX.X, ALU.add).then_inc(ss_ready, 1)
            dve.wait_ge(ss_ready, 1)
            link(dve.scalar_tensor_tensor(work[:, :, :], a[:, :, :], -1.0, rows(k_a), ALU.add, ALU.mult))
            link(dve.scalar_tensor_tensor(key, work[:, :, :], 1.0, key, ALU.add, ALU.mult))
            dve.wait_ge(root_ready, 1)
            link(dve.tensor_scalar(ss[:, :, :], ss[:, :, :], 1e-12, None, ALU.max))
            link(dve.reciprocal(ss[:, :, :], ss[:, :, :]))
            for t in range(LT):
                bt = B[:, t, :].rearrange("p (h d) -> p h d", d=64)
                link(dve.tensor_tensor(bt, bt, ss[:, t, :].unsqueeze(2).to_broadcast([P, RW_H, 64]), ALU.mult))
            dve.wait_ge(before_ready, 1)
            link(dve.tensor_tensor(Q[:, :, :], Q[:, :, :], B[:, :, :], ALU.mult))
            link(dve.tensor_tensor(B[:, :, :], B[:, :, :], a[:, :, :], ALU.mult))
            link(dve.tensor_tensor(B[:, :, :], B[:, :, :], inv[:, :, :], ALU.mult))
            link(dve.tensor_tensor(K[:, :, :], key, inv[:, :, :], ALU.mult))
            link(dve.tensor_tensor(R[:, :, :], R[:, :, :], r, ALU.mult))
            link(dve.tensor_tensor(work[:, :, :], r, key, ALU.mult))
            link(dve.tensor_tensor(work[:, :, :], work[:, :, :], rows(r_k), ALU.mult))
            link(dve.tensor_reduce(bonus[:, :, :], heads(work[:, :, :]), AX.X, ALU.add))


def rw_transposes(k, Q, R, K, B, T4):
    nc = k.nc
    ctx, sb, ps, sem = stage(k, "rw_t")
    with ctx:
        bank = ps("bank", [P, 4, 512])
        flipped, taken = sem("flipped"), sem("taken")
        block = ctx.enter_context(nc.Block())
        jobs = [(p, t) for p in range(RW_PAIRS) for t in range(LT)]

        @block.tensor
        def _(pe):
            for n, (p, t) in enumerate(jobs):
                if n >= 4:
                    pe.wait_ge(taken, n - 3)
                for i, src in enumerate((Q, R, K, B)):
                    last = pe.transpose(bank[:, n % 4, i * P:(i + 1) * P], src[:, t, p * P:(p + 1) * P], k.const("ident"))
                last.then_inc(flipped, 1)

        @block.vector
        def _(dve):
            for n, (p, t) in enumerate(jobs):
                dve.wait_ge(flipped, n + 1)
                dve.tensor_copy(T4[:, p, t].rearrange("p i n -> p (i n)"), bank[:, n % 4, :]).then_inc(taken, 1)


def rw_solve(k, z, Q, K, B, T4, GT, MT, N, y):
    nc = k.nc
    ctx, sb, ps, sem = stage(k, "solve")
    NB = RW_H // 2
    LEV = 6
    STREAMS = range(2)
    with ctx:
        A = [sb(f"A{s}", [P, NB, 4, P]) for s in STREAMS]
        T, TT, LmT, P1, UZ = ([sb(f"{name}{s}", [P, NB, P]) for s in STREAMS] for name in ("T", "TT", "LmT", "P1", "UZ"))
        X = [sb(f"X{s}", [P, NB, 64]) for s in STREAMS]
        prod = [ps(f"prod{s}", [P, 4, 512]) for s in STREAMS]
        t1, t2, pa, pb = ([prod[s][:, i, :] for s in STREAMS] for i in range(4))
        pe_done, dve_done, act_done, pool_done, first_level = (
            [sem(f"{name}{s}") for s in STREAMS] for name in ("pe_done", "dve_done", "act_done", "pool_done", "first_level"))
        block = ctx.enter_context(nc.Block())
        eye = k.const("ident").unsqueeze(1).to_broadcast([P, NB, P])

        def lev(n):
            return k.const(f"rw_lev{n}").unsqueeze(1).to_broadcast([P, NB, P])

        def flat(t):
            return t[:, :, :].rearrange("p b n -> p (b n)")

        PE_N, DVE_N, ACT_N, POOL_N = 2 + (3 * (LEV - 1) - 1) + 5, 3 + (2 * (LEV - 1) - 1) + 6, (LEV - 1) + 2, LEV - 1

        def head(s, b):
            h = s * NB + b
            return h, h // 2, slice((h % 2) * 64, (h % 2) * 64 + 64), slice(h * 64, h * 64 + 64)

        def values(s, b):
            h = s * NB + b
            return slice(2 * RW_D + h * 64, 2 * RW_D + (h + 1) * 64)

        @block.tensor
        def _(pe):
            for t in range(LT):
                d0, a0 = t * DVE_N, t * ACT_N
                for s in STREAMS:
                    if t:
                        pe.wait_ge(dve_done[s], d0)
                        pe.wait_ge(act_done[s], a0)
                    for b in range(NB):
                        h, p, d, cols = head(s, b)
                        qr = T4[d, p, t, 0:2].rearrange("p i n -> p (i n)")
                        pe.matmul(prod[s][:, b, 0:256], T4[d, p, t, 2, :], qr, start=True, stop=True)
                        last = pe.matmul(prod[s][:, b, 256:512], T4[d, p, t, 3, :], qr, start=True, stop=True)
                    last.then_inc(pe_done[s], 1)
                for s in STREAMS:
                    pe.wait_ge(dve_done[s], d0 + 2)
                    for b in range(NB):
                        last = pe.transpose(t1[s][:, b * P:(b + 1) * P], TT[s][:, b, :], k.const("ident"))
                    last.then_inc(pe_done[s], 1)
                for v in range(1, LEV):
                    for s in STREAMS:
                        pe.wait_ge(pool_done[s], t * POOL_N + v)
                        pe.wait_ge(dve_done[s], d0 + 3 + 2 * (v - 1))
                        for b in range(NB):
                            last = pe.matmul(pa[s][:, b * P:(b + 1) * P], LmT[s][:, b, :], T[s][:, b, :], start=True, stop=True)
                        last.then_inc(pe_done[s], 1)
                    for s in STREAMS:
                        pe.wait_ge(act_done[s], a0 + v)
                        for b in range(NB):
                            last = pe.matmul(t2[s][:, b * P:(b + 1) * P], P1[s][:, b, :], TT[s][:, b, :], start=True, stop=True)
                        last.then_inc(pe_done[s], 1)
                        if v < LEV - 1:
                            for b in range(NB):
                                last = pe.matmul(t1[s][:, b * P:(b + 1) * P], TT[s][:, b, :], P1[s][:, b, :], start=True, stop=True)
                            last.then_inc(pe_done[s], 1)
                for s in STREAMS:
                    for b in range(NB):
                        last = pe.matmul(pb[s][:, b * 64:(b + 1) * 64], A[s][:, b, 0, :], z[:, t, values(s, b)], start=True, stop=True)
                    last.then_inc(pe_done[s], 1)
                for s in STREAMS:
                    pe.wait_ge(dve_done[s], d0 + 3 + 2 * (LEV - 1) - 1)
                    pe.wait_ge(act_done[s], a0 + LEV)
                    for b in range(NB):
                        h, p, d, cols = head(s, b)
                        pe.matmul(pa[s][:, b * P:b * P + 64], TT[s][:, b, :], Q[:, t, cols], start=True, stop=True)
                        last = pe.matmul(pa[s][:, b * P + 64:(b + 1) * P], TT[s][:, b, :], X[s][:, b, :], start=True, stop=True)
                    last.then_inc(pe_done[s], 1)
                for s in STREAMS:
                    pe.wait_ge(act_done[s], a0 + LEV + 1)
                    for b in range(NB):
                        h, p, d, cols = head(s, b)
                        last = pe.matmul(t1[s][d, (b // 2) * P:(b // 2 + 1) * P], UZ[s][:, b, 0:64], A[s][:, b, 3, :], start=True, stop=True)
                    last.then_inc(pe_done[s], 1)
                    for b in range(NB):
                        place = t2[s][:, b * 64:(b + 1) * 64]
                        pe.matmul(place, A[s][:, b, 3, :], UZ[s][:, b, 64:P], start=True, stop=False)
                        last = pe.matmul(place, A[s][:, b, 1, :], z[:, t, values(s, b)], start=False, stop=True)
                    last.then_inc(pe_done[s], 1)
                    for c in range(2):
                        rows = slice(c * 64, c * 64 + 64)
                        for b in range(NB):
                            h, p, d, cols = head(s, b)
                            q = b // 2
                            m_place, n_place = (prod[s][d, 2 + c, i * 128 + q * 64:i * 128 + (q + 1) * 64] for i in range(2))
                            pe.matmul(m_place, UZ[s][rows, b, 0:64], B[rows, t, cols], start=True, stop=True)
                            pe.matmul(n_place, B[rows, t, cols], UZ[s][rows, b, 64:P], start=True, stop=False)
                            last = pe.matmul(n_place, K[rows, t, cols], z[rows, t, values(s, b)], start=False, stop=True)
                    last.then_inc(pe_done[s], 1)

        @block.gpsimd
        def _(pool):
            for t in range(LT):
                for v in range(1, LEV):
                    for s in STREAMS:
                        if v == 1:
                            pool.wait_ge(dve_done[s], t * DVE_N + 1)
                        else:
                            pool.wait_ge(pe_done[s], t * PE_N + 2 + 3 * (v - 2) + 1)
                        pool.tensor_tensor(LmT[s][:, :, :], A[s][:, :, 2, :], lev(v), ALU.mult).then_inc(pool_done[s], 1)

        @block.scalar
        def _(act):
            for t in range(LT):
                e = t * PE_N
                for v in range(1, LEV):
                    for s in STREAMS:
                        act.wait_ge(pe_done[s], e + 2 + 3 * (v - 1) + 1)
                        act.activation(flat(P1[s]), pa[s], ACT.Copy).then_inc(act_done[s], 1)
                i = e + 2 + 3 * (LEV - 1) - 1
                for s in STREAMS:
                    act.wait_ge(pe_done[s], i + 1)
                    act.activation(flat(X[s]), pb[s][:, 0:NB * 64], ACT.Copy).then_inc(act_done[s], 1)
                for s in STREAMS:
                    act.wait_ge(pe_done[s], i + 2)
                    act.activation(flat(UZ[s]), pa[s], ACT.Copy, scale=-1.0).then_inc(act_done[s], 1)

        @block.vector
        def _(dve):
            mask = k.const("rw_mask").unsqueeze(1).to_broadcast([P, 2 * NB, 256])
            for t in range(LT):
                e, d0 = t * PE_N, t * DVE_N
                for s in STREAMS:
                    if t:
                        dve.wait_ge(pool_done[s], t * POOL_N)
                    dve.wait_ge(pe_done[s], e + 1)
                    dve.tensor_tensor(A[s][:, :, :, :].rearrange("p b (i m) n -> p (b i) (m n)", m=2),
                                      prod[s][:, :, :].rearrange("p b (i n) -> p (b i) n", n=256), mask, ALU.mult).then_inc(dve_done[s], 1)
                    dve.wait_ge(dve_done[s], d0 + 1)
                    dve.tensor_tensor(TT[s][:, :, :], A[s][:, :, 2, :], lev(0), ALU.mult).then_inc(first_level[s], 1)
                    dve.wait_ge(first_level[s], t + 1)
                    dve.tensor_tensor(TT[s][:, :, :], eye, TT[s][:, :, :], ALU.subtract).then_inc(dve_done[s], 1)
                for s in STREAMS:
                    dve.wait_ge(pe_done[s], e + 2)
                    dve.tensor_copy(flat(T[s]), t1[s]).then_inc(dve_done[s], 1)
                for v in range(1, LEV):
                    i = e + 2 + 3 * (v - 1)
                    for s in STREAMS:
                        if v < LEV - 1:
                            dve.wait_ge(pe_done[s], i + 3)
                            dve.tensor_tensor(flat(T[s]), flat(T[s]), t1[s], ALU.subtract).then_inc(dve_done[s], 1)
                        else:
                            dve.wait_ge(pe_done[s], i + 2)
                        dve.tensor_tensor(flat(TT[s]), flat(TT[s]), t2[s], ALU.subtract).then_inc(dve_done[s], 1)
                i = e + 2 + 3 * (LEV - 1) - 1
                for s in STREAMS:
                    pair = slice(s * 2, s * 2 + 2)
                    dve.wait_ge(pe_done[s], i + 3)
                    dve.tensor_tensor(GT[:, pair, t, :], t1[s][:, 0:256].rearrange("p (a n) -> p a n", n=P), T4[:, pair, t, 1, :],
                                      ALU.add).then_inc(dve_done[s], 1)
                    dve.wait_ge(pe_done[s], i + 4)
                    dve.tensor_copy(y[:, t, s * 256:(s + 1) * 256], t2[s][:, 0:256]).then_inc(dve_done[s], 1)
                    dve.wait_ge(pe_done[s], i + 5)
                    for c in range(2):
                        both = prod[s][:, 2 + c, 0:256].rearrange("p (m a n) -> p m a n", m=2, n=64)
                        dve.tensor_tensor(MT[:, pair, 2 * t + c, :], both[:, 0],
                                          k.const("rw_eye").unsqueeze(1).to_broadcast([P, 2, 64]), ALU.add).then_inc(dve_done[s], 1)
                        dve.tensor_copy(N[:, pair, 2 * t + c, :], both[:, 1]).then_inc(dve_done[s], 1)


def rw_states(k, MT, N, D_next, GT, y):
    nc = k.nc
    ctx, sb, ps, sem = stage(k, "states")
    with ctx:
        S = sb("S", [P, RW_CH, RW_PAIRS, 64])
        nxt = ps("nxt", [P, 2, 512])
        out = ps("out", [P, 4, 512])
        moved, s_ready, y_ready, y_done, step = (sem(x) for x in ("moved", "s_ready", "y_ready", "y_done", "step"))
        block = ctx.enter_context(nc.Block())

        @block.tensor
        def _(pe):
            def add_rows(t):
                pe.wait_ge(s_ready, 2 * t + 1)
                if t >= 2:
                    pe.wait_ge(y_done, 2 * (t - 1))
                for c in range(2 * t, 2 * t + 2):
                    if c == 0:
                        continue
                    rows = slice((c % 2) * 64, (c % 2) * 64 + 64)
                    for hp in range(2):
                        d = slice(hp * 64, hp * 64 + 64)
                        for p in range(RW_PAIRS):
                            last = pe.matmul(out[rows, 2 * (t % 2) + hp, p * 64:(p + 1) * 64], GT[d, p, t, rows], S[d, c, p, :],
                                             start=True, stop=True)
                last.then_inc(y_ready, 1)

            for c in range(1, RW_CH - 1):
                pe.wait_ge(s_ready, c)
                for hp in range(2):
                    d = slice(hp * 64, hp * 64 + 64)
                    for p in range(RW_PAIRS):
                        last = pe.matmul(nxt[d, hp, p * 64:(p + 1) * 64], MT[d, p, c, :], S[d, c, p, :], start=True, stop=True)
                last.then_inc(moved, 1)
            for t in range(LT):
                add_rows(t)

        @block.vector
        def _(dve):
            link = Steps(dve, step)

            def spread(c):
                return D_next[:, :, c].unsqueeze(2).to_broadcast([P, RW_PAIRS, 64])

            for c in range(RW_CH - 1):
                if c == 0:
                    dve.tensor_tensor(S[:, 1], N[:, :, 0, :], spread(0), ALU.mult).then_inc(s_ready, 1)
                    continue
                dve.wait_ge(moved, c)
                for hp in range(2):
                    d = slice(hp * 64, hp * 64 + 64)
                    link(dve.tensor_tensor(S[d, c + 1], nxt[d, hp, 0:256].rearrange("p (a n) -> p a n", n=64), N[d, :, c, :], ALU.add))
                dve.tensor_tensor(S[:, c + 1], S[:, c + 1], spread(c), ALU.mult).then_inc(s_ready, 1)
            for t in range(LT):
                dve.wait_ge(y_ready, t + 1)
                rows = slice(64, P) if t == 0 else slice(0, P)
                for hp in range(2):
                    yv = y[rows, t, :].rearrange("p (a h n) -> p a h n", h=2, n=64)[:, :, hp, :]
                    dve.tensor_tensor(yv, yv, out[rows, 2 * (t % 2) + hp, 0:256].rearrange("p (a n) -> p a n", n=64),
                                      ALU.add).then_inc(y_done, 1)
            dve.wait_ge(y_done, 2 * LT)


def rw_finish(k, y, z, g, bonus):
    nc = k.nc
    ctx, sb, ps, sem = stage(k, "rw_fin")
    with ctx:
        gn_w, gn_b = sb("gn_w", [P, RW_D]), sb("gn_b", [P, RW_D])
        work = sb("work", [P, LT, RW_D])
        mean, var = sb("mean", [P, LT, RW_H]), sb("var", [P, LT, RW_H])
        loaded, var_ready, root_ready, bonus_ready, step = (sem(x) for x in ("loaded", "var_ready", "root_ready", "bonus_ready", "step"))
        block = ctx.enter_context(nc.Block())

        def heads(t):
            return t.rearrange("p (h d) -> p h d", d=64)

        def spread(s, t):
            return s[:, t, :].unsqueeze(2).to_broadcast([P, RW_H, 64])

        def rows(t):
            return t[:, :].unsqueeze(1).to_broadcast([P, LT, RW_D])

        @block.sync
        def _(sp):
            sp.dma_start(gn_w[:, :], k.dram["rw_gn_w_2"][0:1, :].to_broadcast([P, RW_D])).then_inc(loaded, 16)
            sp.dma_start(gn_b[:, :], k.dram["rw_gn_b_2"][0:1, :].to_broadcast([P, RW_D])).then_inc(loaded, 16)

        @block.gpsimd
        def _(pool):
            for t in range(LT):
                v = z[:, t, 2 * RW_D:3 * RW_D]
                pool.tensor_tensor(heads(v), heads(v), spread(bonus, t), ALU.mult).then_inc(bonus_ready, 1)

        @block.scalar
        def _(act):
            act.wait_ge(var_ready, 1)
            act.activation(var[:, :, :], var[:, :, :], ACT.Sqrt, scale=1.0 / 64, bias=k.const("gn_eps")).then_inc(root_ready, 1)

        @block.vector
        def _(dve):
            link = Steps(dve, step)
            link(dve.tensor_reduce(mean[:, :, :], y[:, :, :].rearrange("p t (h d) -> p t h d", d=64), AX.X, ALU.add))
            link(dve.tensor_scalar(mean[:, :, :], mean[:, :, :], 1.0 / 64, None, ALU.mult))
            for t in range(LT):
                link(dve.tensor_tensor(heads(y[:, t, :]), heads(y[:, t, :]), spread(mean, t), ALU.subtract))
            link(dve.tensor_tensor(work[:, :, :], y[:, :, :], y[:, :, :], ALU.mult))
            dve.tensor_reduce(var[:, :, :], work[:, :, :].rearrange("p t (h d) -> p t h d", d=64), AX.X, ALU.add).then_inc(var_ready, 1)
            dve.wait_ge(root_ready, 1)
            link(dve.reciprocal(var[:, :, :], var[:, :, :]))
            for t in range(LT):
                link(dve.tensor_tensor(heads(y[:, t, :]), heads(y[:, t, :]), spread(var, t), ALU.mult))
            dve.wait_ge(loaded, 32)
            link(dve.tensor_tensor(y[:, :, :], y[:, :, :], rows(gn_w), ALU.mult))
            link(dve.tensor_tensor(y[:, :, :], y[:, :, :], rows(gn_b), ALU.add))
            dve.wait_ge(bonus_ready, LT)
            link(dve.tensor_tensor(y[:, :, :], y[:, :, :], z[:, :, 2 * RW_D:3 * RW_D], ALU.add))
            link(dve.tensor_tensor(y[:, :, :], y[:, :, :], g[:, :, :], ALU.mult))


def mla_rows(k, down, qn, kvn, cT, sT, krT):
    nc = k.nc
    ctx, sb, ps, sem = stage(k, "mla_rows")
    H = MLA_ROPE // 2
    TWO_PI = 2 * np.pi
    PART1 = 6.28125
    PART2 = 0.0019350051879882812
    PART3 = TWO_PI - PART1 - PART2
    ROUND = 12582912.0
    with ctx:
        pos_i, pos = sb("pos_i", [P, LT], I32), sb("pos", [P, LT])
        ang, turns, sin, cos, half = (sb(n, [P, LT, H]) for n in ("ang", "turns", "sin", "cos", "half"))
        table = sb("table", [P, 3, LT, MLA_QK])
        square = sb("square", [P, MLA_Q])
        ss, rstd = sb("ss", [P, 2, LT]), sb("rstd", [P, 2, LT])
        tmp = sb("tmp", [P, 2, LT, H])
        bank = ps("bank", [P, 3, 512])
        loaded, reduced, sined, root_ready, table_ready, flipped, step, act_step = (
            sem(x) for x in ("loaded", "reduced", "sined", "root_ready", "table_ready", "flipped", "step", "act_step"))
        block = ctx.enter_context(nc.Block())
        parts = (down[:, :, 0:MLA_Q], down[:, :, MLA_Q:MLA_Q + MLA_KV])
        kr = down[:, :, MLA_Q + MLA_KV:MLA_Q + MLA_KV + MLA_ROPE]

        @block.sync
        def _(sp):
            sp.dma_start(pos_i[:, :], k.dram["positions_2"].rearrange("a (t p) -> p (a t)", p=P),
                         allow_slow_non_contiguous=True).then_inc(loaded, 16)

        @block.scalar
        def _(act):
            link = Steps(act, act_step)
            for i, (x, n) in enumerate(zip(parts, (MLA_Q, MLA_KV))):
                for t in range(LT):
                    link(act.activation(square[:, 0:n], x[:, t, :], ACT.Square, accum_out=ss[:, i, t:t + 1]))
                act.activation(rstd[:, i, :], ss[:, i, :], ACT.Sqrt, scale=1.0 / n, bias=k.const("eps")).then_inc(root_ready, 1)
            act.wait_ge(reduced, 1)
            act.activation(sin[:, :, :], ang[:, :, :], ACT.Sin).then_inc(sined, 1)
            act.activation(half[:, :, :], ang[:, :, :], ACT.Sin, scale=0.5).then_inc(sined, 1)

        @block.vector
        def _(dve):
            link = Steps(dve, step)
            link(dve.memset(table[:, 0], 1.0))
            link(dve.memset(table[:, 1:3], 0.0))
            dve.wait_ge(loaded, 16)
            link(dve.tensor_copy(pos[:, :], pos_i[:, :]))
            link(dve.tensor_tensor(ang[:, :, :], pos[:, :].unsqueeze(2).to_broadcast([P, LT, H]),
                                   k.const("mla_inv").unsqueeze(1).to_broadcast([P, LT, H]), ALU.mult))
            link(dve.tensor_scalar(turns[:, :, :], ang[:, :, :], 1.0 / TWO_PI, ROUND, ALU.mult, ALU.add))
            link(dve.tensor_scalar(turns[:, :, :], turns[:, :, :], -ROUND, None, ALU.add))
            link(dve.scalar_tensor_tensor(ang[:, :, :], turns[:, :, :], -PART1, ang[:, :, :], ALU.mult, ALU.add))
            link(dve.scalar_tensor_tensor(ang[:, :, :], turns[:, :, :], -PART2, ang[:, :, :], ALU.mult, ALU.add))
            link(dve.scalar_tensor_tensor(ang[:, :, :], turns[:, :, :], -PART3, ang[:, :, :], ALU.mult, ALU.add))
            link(dve.tensor_scalar(ang[:, :, :], ang[:, :, :], float(np.float32(np.pi)), -float(np.float32(np.pi)), ALU.min, ALU.max))
            dve.nop().then_inc(reduced, 1)
            dve.wait_ge(sined, 2)
            link(dve.tensor_tensor(cos[:, :, :], half[:, :, :], half[:, :, :], ALU.mult))
            link(dve.tensor_scalar(cos[:, :, :], cos[:, :, :], -2.0, 1.0, ALU.mult, ALU.add))
            first, second = slice(MLA_NOPE, MLA_NOPE + H), slice(MLA_NOPE + H, MLA_QK)
            for where in (first, second):
                link(dve.tensor_copy(table[:, 0, :, where], cos[:, :, :]))
                link(dve.tensor_copy(table[:, 1, :, where], sin[:, :, :]))
            k1, k2 = kr[:, :, 0:H], kr[:, :, H:2 * H]
            for where, a, b, op in ((first, k1, k2, ALU.subtract), (second, k2, k1, ALU.add)):
                link(dve.tensor_tensor(tmp[:, 0], a, cos[:, :, :], ALU.mult))
                link(dve.tensor_tensor(tmp[:, 1], b, sin[:, :, :], ALU.mult))
                link(dve.tensor_tensor(table[:, 2, :, where], tmp[:, 0], tmp[:, 1], op))
            dve.nop().then_inc(table_ready, 1)
            dve.wait_ge(root_ready, 2)
            link(dve.reciprocal(rstd[:, :, :], rstd[:, :, :]))
            for i, (x, dst) in enumerate(zip(parts, (qn, kvn))):
                for t in range(LT):
                    link(dve.tensor_scalar(dst[:, t, :], x[:, t, :], rstd[:, i, t:t + 1], None, ALU.mult))
            dve.wait_ge(flipped, 1)
            for i, dst in enumerate((cT, sT, krT)):
                link(dve.tensor_copy(dst[:, :], bank[0:MLA_QK, i, :]))

        @block.tensor
        def _(pe):
            pe.wait_ge(table_ready, 1)
            for i in range(3):
                for t in range(LT):
                    last = pe.transpose(bank[0:MLA_QK, i, t * P:(t + 1) * P], table[:, i, t, :], k.const("ident"))
            last.then_inc(flipped, 1)


def mla_up(k, qnT, kvnT, cT, sT, krT, qT, kT, v):
    nc = k.nc
    ctx, sb, ps, sem = stage(k, "mla_up")
    NQ, NKV = MLA_Q // P, MLA_KV // P
    with ctx:
        wq, wkv = sb("wq", [P, NQ, MLA_H * MLA_QK]), sb("wkv", [P, NKV, MLA_H * 128])
        raw = sb("raw", [MLA_QK, 2, L])
        turned = sb("turned", [MLA_QK, 2, L])
        pq, psw, pk, pv = ps("pq", [P, 2, 512]), ps("psw", [P, 2, 512]), ps("pk", [P, 2, 512]), ps("pv", [P, 2, 512])
        loaded, q_ready, raw_ready, swapped, turned_ready, q_done, k_ready, k_taken, kr_ready, v_ready, v_taken, pool_step = (
            sem(x) for x in ("loaded", "q_ready", "raw_ready", "swapped", "turned_ready", "q_done", "k_ready", "k_taken", "kr_ready", "v_ready", "v_taken", "pool_step"))
        block = ctx.enter_context(nc.Block())

        @block.sync
        def _(sp):
            sp.dma_start(wq[:, :, :], k.dram["mla_w_q_up_2"][0].rearrange("(k p) n -> p k n", p=P)).then_inc(loaded, 16)
            sp.dma_start(wkv[:, :, :], k.dram["mla_w_kv_up_2"][0].rearrange("(k p) n -> p k n", p=P)).then_inc(loaded, 16)

        @block.gpsimd
        def _(pool):
            for h in range(MLA_H):
                pool.tensor_copy(kT[MLA_NOPE:MLA_QK, h, :], krT[MLA_NOPE:MLA_QK, :]).then_inc(kr_ready, 1)
            pool.wait_ge(kr_ready, MLA_H)

        @block.tensor
        def _(pe):
            pe.wait_ge(loaded, 32)

            def swap(h):
                pe.wait_ge(raw_ready, h + 1)
                if h >= 2:
                    pe.wait_ge(turned_ready, h - 1)
                pe.matmul(psw[0:MLA_QK, h % 2, :], k.const("mla_swap", MLA_QK)[:, 0:MLA_QK], raw[:, h % 2, :], start=True,
                          stop=True).then_inc(swapped, 1)

            for h in range(MLA_H):
                if h >= 2:
                    pe.wait_ge(raw_ready, h - 1)
                for j in range(NQ):
                    last = pe.matmul(pq[0:MLA_QK, h % 2, :], wq[:, j, h * MLA_QK:(h + 1) * MLA_QK], qnT[:, j, :], start=(j == 0), stop=(j == NQ - 1))
                last.then_inc(q_ready, 1)
                if h >= 2:
                    pe.wait_ge(k_taken, h - 1)
                for j in range(NKV):
                    last = pe.matmul(pk[0:MLA_NOPE, h % 2, :], wkv[:, j, h * 128:h * 128 + MLA_NOPE], kvnT[:, j, :], start=(j == 0), stop=(j == NKV - 1))
                last.then_inc(k_ready, 1)
                if h:
                    swap(h - 1)
            swap(MLA_H - 1)
            for t in range(LT):
                if t >= 2:
                    pe.wait_ge(v_taken, t - 1)
                for j in range(NKV):
                    last = pe.matmul(pv[:, t % 2, :], kvnT[:, j, t * P:(t + 1) * P],
                                     wkv[:, j, :].rearrange("p (h n) -> p h n", n=128)[:, :, MLA_NOPE:128], start=(j == 0), stop=(j == NKV - 1))
                last.then_inc(v_ready, 1)

        @block.scalar
        def _(act):
            for h in range(MLA_H):
                act.wait_ge(q_ready, h + 1)
                if h >= 2:
                    act.wait_ge(q_done, h - 1)
                act.activation(raw[:, h % 2, :], pq[0:MLA_QK, h % 2, :], ACT.Copy).then_inc(raw_ready, 1)
                act.wait_ge(k_ready, h + 1)
                act.activation(kT[0:MLA_NOPE, h, :], pk[0:MLA_NOPE, h % 2, :], ACT.Copy).then_inc(k_taken, 1)
            for t in range(LT):
                act.wait_ge(v_ready, t + 1)
                act.activation(v[:, t, :], pv[:, t % 2, :], ACT.Copy).then_inc(v_taken, 1)
            act.wait_ge(v_taken, LT)

        @block.vector
        def _(dve):
            for h in range(MLA_H):
                dve.wait_ge(swapped, h + 1)
                if h >= 2:
                    dve.wait_ge(q_done, h - 1)
                dve.tensor_tensor(turned[:, h % 2, :], psw[0:MLA_QK, h % 2, :], sT[:, :], ALU.mult).then_inc(turned_ready, 1)
                dve.tensor_tensor(qT[:, h, :], raw[:, h % 2, :], cT[:, :], ALU.mult).then_inc(pool_step, 1)
                dve.wait_ge(turned_ready, h + 1)
                dve.wait_ge(pool_step, h + 1)
                dve.tensor_tensor(qT[:, h, :], qT[:, h, :], turned[:, h % 2, :], ALU.add).then_inc(q_done, 1)
            dve.wait_ge(q_done, MLA_H)


def causal_attention(k, qT, kT, v, o):
    nc = k.nc
    ctx, sb, ps, sem = stage(k, "mla")
    SCALE = MLA_QK ** -0.5
    units = [(h, t) for h in range(MLA_H) for t in range(LT)]
    with ctx:
        s, p, pT = sb("s", [P, 2, L]), sb("p", [P, 2, L]), sb("pT", [P, 2, L])
        top, total, inv = sb("top", [P, 2]), sb("total", [P, 4]), sb("inv", [P, 2])
        score, flip, out = ps("score", [P, 2, 512]), ps("flip", [P, 2, 512]), ps("out", [P, 2, 512])
        scored, masked, topped, exped, flipped, flip_taken, valued, normed, step = (
            sem(x) for x in ("scored", "masked", "topped", "exped", "flipped", "flip_taken", "valued", "normed", "step"))
        block = ctx.enter_context(nc.Block())

        @block.tensor
        def _(pe):
            def scores(u):
                h, t = units[u]
                if u >= 2:
                    pe.wait_ge(masked, u - 1)
                pe.matmul(score[:, u % 2, 0:(t + 1) * P], qT[:, h, t * P:(t + 1) * P], kT[:, h, 0:(t + 1) * P], start=True,
                          stop=True).then_inc(scored, 1)

            def turn(u):
                h, t = units[u]
                b = u % 2
                pe.wait_ge(exped, u + 1)
                if u >= 2:
                    pe.wait_ge(flip_taken, u - 1)
                for j in range(t + 1):
                    last = pe.transpose(flip[:, b, j * P:(j + 1) * P], p[:, b, j * P:(j + 1) * P], k.const("ident"))
                last.then_inc(flipped, 1)

            def values(u):
                h, t = units[u]
                b = u % 2
                pe.wait_ge(flip_taken, u + 1)
                if u >= 2:
                    pe.wait_ge(normed, u - 1)
                for j in range(t + 1):
                    last = pe.matmul(out[:, b, 0:64], pT[:, b, j * P:(j + 1) * P], v[:, j, h * 64:(h + 1) * 64], start=(j == 0), stop=(j == t))
                last.then_inc(valued, 1)

            scores(0)
            scores(1)
            for u in range(len(units)):
                turn(u)
                if u + 2 < len(units):
                    scores(u + 2)
                if u:
                    values(u - 1)
            values(len(units) - 1)

        @block.scalar
        def _(act):
            def weights(u):
                h, t = units[u]
                n = (t + 1) * P
                act.wait_ge(topped, u + 1)
                if u >= 2:
                    act.wait_ge(flipped, u - 1)
                act.activation(p[:, u % 2, 0:n], s[:, u % 2, 0:n], ACT.Exp, scale=SCALE, bias=top[:, u % 2:u % 2 + 1],
                               accum_out=total[:, u % 4:u % 4 + 1]).then_inc(exped, 1)

            weights(0)
            for u, (h, t) in enumerate(units):
                if u + 1 < len(units):
                    weights(u + 1)
                act.wait_ge(flipped, u + 1)
                act.activation(pT[:, u % 2, 0:(t + 1) * P], flip[:, u % 2, 0:(t + 1) * P], ACT.Copy).then_inc(flip_taken, 1)

        @block.vector
        def _(dve):
            link = Steps(dve, step)

            def highest(u):
                h, t = units[u]
                b = u % 2
                dve.wait_ge(scored, u + 1)
                if u >= 2:
                    dve.wait_ge(exped, u - 1)
                if t:
                    link(dve.tensor_copy(s[:, b, 0:t * P], score[:, b, 0:t * P]))
                dve.tensor_tensor(s[:, b, t * P:(t + 1) * P], score[:, b, t * P:(t + 1) * P], k.const("mla_causal"), ALU.add).then_inc(masked, 1)
                dve.wait_ge(masked, u + 1)
                link(dve.tensor_reduce(top[:, b:b + 1], s[:, b, 0:(t + 1) * P], AX.X, ALU.max))
                dve.tensor_scalar(top[:, b:b + 1], top[:, b:b + 1], -SCALE, None, ALU.mult).then_inc(topped, 1)

            highest(0)
            highest(1)
            for u, (h, t) in enumerate(units):
                b = u % 2
                if u + 2 < len(units):
                    highest(u + 2)
                dve.wait_ge(exped, u + 1)
                link(dve.reciprocal(inv[:, b:b + 1], total[:, u % 4:u % 4 + 1]))
                dve.wait_ge(valued, u + 1)
                dve.tensor_scalar(o[:, t, h * 64:(h + 1) * 64], out[:, b, 0:64], inv[:, b:b + 1], None, ALU.mult).then_inc(normed, 1)
            dve.wait_ge(normed, len(units))


def latent_attention(k, hT, o, w_down, ahead, then):
    nc = k.nc
    vec2 = k.second

    def tile(scope, name, shape):
        return scope.enter_context(nc.sbuf_tensor(name, shape, F32))

    with ExitStack() as s:
        load_constants(k, s, "mla")
        qT, kT, v = tile(s, "mla_qT", [MLA_QK, MLA_H, L]), tile(s, "mla_kT", [MLA_QK, MLA_H, L]), tile(s, "mla_v", [P, LT, MLA_H * 64])
        with ExitStack() as s1:
            cT, sT, krT = (tile(s1, n, [MLA_QK, L]) for n in ("mla_cT", "mla_sT", "mla_krT"))
            qnT, kvnT = tile(s1, "mla_qnT", [P, 3, L]), tile(s1, "mla_kvnT", [P, 2, L])
            with ExitStack() as s2:
                n = MLA_Q + MLA_KV + MLA_ROPE
                down = tile(s2, "mla_down", [P, LT, n])
                qn, kvn = tile(s2, "mla_qn", [P, LT, MLA_Q]), tile(s2, "mla_kvn", [P, LT, MLA_KV])
                project_rows(k, "p_mla", w_down, KD, hT, down, 2, n // 2, ahead=ahead, then=then)
                mla_rows(k, down, qn, kvn, cT, sT, krT)
                transpose_rows(k, "mla_qn_t", qn, LT, 3, qnT, vec2[:, W2_QA:W2_QA + 3])
                transpose_rows(k, "mla_kvn_t", kvn, LT, 2, kvnT, vec2[:, W2_KVA:W2_KVA + 2])
            mla_up(k, qnT, kvnT, cT, sT, krT, qT, kT, v)
        causal_attention(k, qT, kT, v, o)


def second_mixer(k, x_in, x_out, dump=None):
    nc = k.nc
    dump = dump or (lambda name, ap: None)
    vec2 = k.second
    w_in = k.dram["w_in_2"][0]

    def tile(scope, name, shape):
        return scope.enter_context(nc.sbuf_tensor(name, shape, F32))

    def cols(name):
        return k.dram[name].rearrange("a (n p) -> (a n) p", p=P)

    column_vectors(k, "vec_2", [cols("mix_norm_g_2"), cols("ffn_norm_g_2"), cols("mla_g_qa_2"), cols("mla_g_kva_2"),
                                cols("rw_mu_2")], vec2)
    w_gate_rw, w_gate_mla = w_in[:, COL_G2:COL_G2 + D], w_in[:, COL_G2 + D:COL_G2 + 2 * D]
    w_rkv = w_in[:, 0:3 * RW_D]
    n_down = MLA_Q + MLA_KV + MLA_ROPE
    w_down = w_in[:, COL_MQ:COL_MQ + n_down]
    with ExitStack() as outer:
        uT = tile(outer, "u2T", [P, KD, L])
        with ExitStack() as mid:
            hT, y = tile(mid, "h2mT", [P, KD, L]), tile(mid, "rw_y", [P, LT, RW_D])
            with ExitStack() as s:
                z = tile(s, "rw_z", [P, LT, 3 * RW_D])
                with ExitStack() as s1:
                    ahead = WeightsAhead(k, s1, "ahead_rkv")
                    ahead.start(w_rkv, KD, 384)
                    rows = tile(s1, "x2_rows", [P, LT, D])
                    load(k, "x2r_load", [(rows[:, :, :], rows_view(x_in))])
                    norm_transpose(k, "x2_norm", rows, LT, hT, vec2[:, W2_MIX:W2_MIX + KD])
                    project_rows(k, "p_rkv", w_rkv, KD, hT, z, 4, 384, ahead=ahead)
                g, bonus = tile(s, "rw_g", [P, LT, RW_D]), tile(s, "rw_bonus", [P, LT, RW_H])
                load_constants(k, s, "rw")
                with ExitStack() as s1:
                    Q, R, K_, B = (tile(s1, n, [P, LT, RW_D]) for n in ("rw_Q", "rw_R", "rw_K", "rw_B"))
                    D_next = tile(s1, "rw_D", [P, RW_PAIRS, RW_CH])
                    with ExitStack() as s2:
                        lw, a = tile(s2, "rw_lw", [P, LT, RW_D]), tile(s2, "rw_a", [P, LT, RW_D])
                        rw_lora(k, hT, vec2[:, W2_MU + 12:W2_MU + 14], lw, a, g)
                        rw_shift(k, z)
                        rw_scaled(k, z, lw, a, Q, R, K_, B, D_next, bonus)
                    T4 = tile(s1, "rw_T4", [P, RW_PAIRS, LT, 4, P])
                    rw_transposes(k, Q, R, K_, B, T4)
                    GT = tile(s1, "rw_GT", [P, RW_PAIRS, LT, P])
                    MT, N = tile(s1, "rw_MT", [P, RW_PAIRS, RW_CH, 64]), tile(s1, "rw_N", [P, RW_PAIRS, RW_CH, 64])
                    rw_solve(k, z, Q, K_, B, T4, GT, MT, N, y)
                    rw_states(k, MT, N, D_next, GT, y)
                rw_finish(k, y, z, g, bonus)
                dump("y_rw", y)
            ahead = WeightsAhead(k, mid, "ahead_2")
            ahead.start(w_gate_rw, KD, 512)
            with ExitStack() as s:
                yT = tile(s, "rw_yT", [P, RW_D // P, L])
                transpose_rows(k, "rw_y_t", y, LT, RW_D // P, yT)
                gated_branch(k, "rw_br", w_gate_rw, hT, k.dram["w_branch_rw_2"][0], RW_D // P, yT, uT, add=False, ahead=ahead,
                             then=(w_down, KD, n_down // 2))
            with ExitStack() as s:
                o = tile(s, "mla_o", [P, LT, MLA_H * 64])
                latent_attention(k, hT, o, w_down, ahead, (w_gate_mla, KD, 512))
                dump("y_mla", o)
                oT = tile(s, "mla_oT", [P, 4, L])
                transpose_rows(k, "mla_o_t", o, LT, 4, oT)
                gated_branch(k, "mla_br", w_gate_mla, hT, k.dram["w_branch_mla_2"][0], 4, oT, uT, add=True, ahead=ahead,
                             then=(k.dram["w_out_2"][0], KD, 512))
            with ExitStack() as s:
                x, mix = tile(s, "x3", [P, LT, D]), tile(s, "mix2", [P, LT, D])
                load(k, "x3_load", [(x[:, :, :], rows_view(x_in))])
                project_rows(k, "p_out2", k.dram["w_out_2"][0], KD, uT, mix, 2, ahead=ahead)
                add_rows(k, "add3", x, mix)
                load(k, "x3_store", [(rows_view(x_out), x[:, :, :])])


def add_rows(k, label, x, y):
    ctx, sb, ps, sem = stage(k, label)
    with ctx:
        done = sem("done")
        block = ctx.enter_context(k.nc.Block())

        @block.vector
        def _(dve):
            for t in range(LT):
                dve.tensor_tensor(x[:, t, :], x[:, t, :], y[:, t, :], ALU.add).then_inc(done, 1)
            dve.wait_ge(done, LT)


def choose_experts(k, h3T, rank, gate, rounds):
    nc = k.nc
    ctx, sb, ps, sem = stage(k, "hm_choose")
    E, G, N = HM_E, HM_G, HM_G + HM_E
    with ctx:
        w, bias = sb("w", [P, KD, N]), sb("bias", [P, N])
        logit = sb("logit", [P, LT, N])
        prob = sb("prob", [P, LT, G])
        group, group_off, mark4 = sb("group", [P, LT, G]), sb("group_off", [P, LT, G]), sb("mark4", [P, LT, G])
        top, total, gate_g = sb("top", [P, LT]), sb("total", [P, LT]), sb("gate_g", [P, LT])
        fine, mark = sb("fine", [P, LT, E]), sb("mark", [P, LT, E])
        best = sb("best", [P, 2, LT, E])
        value, share = sb("value", [P, 2, LT]), sb("share", [P, 2, LT])
        chosen = sb("chosen", [P, LT, E])
        most, over = sb("most", [P, 1]), sb("over", [P, L // SLOTS])
        score, count = ps("score", [P, 512]), ps("count", [P, 512])
        loaded, scored, exp_in, exp_out, gap_in, gap_out, chosen_ready, counted, step = (
            sem(x) for x in ("loaded", "scored", "exp_in", "exp_out", "gap_in", "gap_out", "chosen_ready", "counted", "step"))
        block = ctx.enter_context(nc.Block())

        @block.sync
        def _(sp):
            for name, a, n in (("group", 0, G), ("router", G, E)):
                sp.dma_start(w[:, :, a:a + n], k.dram[f"moe_w_{name}_2"][0].rearrange("(k p) n -> p k n", p=P)).then_inc(loaded, 16)
                sp.dma_start(bias[:, a:a + n], k.dram[f"moe_b_{name}_2"][0:1, :].to_broadcast([P, n])).then_inc(loaded, 16)

        @block.tensor
        def _(pe):
            pe.wait_ge(loaded, 64)
            for t in range(LT):
                for j in range(KD):
                    last = pe.matmul(score[:, t * N:(t + 1) * N], h3T[:, j, t * P:(t + 1) * P], w[:, j, :], start=(j == 0), stop=(j == KD - 1))
            last.then_inc(scored, 1)
            pe.wait_ge(chosen_ready, 1)
            for t in range(LT):
                for u in range(t + 1):
                    pe.matmul(count[:, t * E:(t + 1) * E], k.const("upto" if u == t else "ones"), chosen[:, u, :],
                              start=(u == 0), stop=(u == t))
            for u in range(LT):
                last = pe.matmul(count[:, LT * E:(LT + 1) * E], k.const("ones"), chosen[:, u, :], start=(u == 0), stop=(u == LT - 1))
            last.then_inc(counted, 1)

        @block.scalar
        def _(act):
            act.wait_ge(exp_in, 1)
            act.activation(prob[:, :, :], prob[:, :, :], ACT.Exp).then_inc(exp_out, 1)
            act.wait_ge(gap_in, 1)
            act.activation(share[:, 1, :], share[:, 1, :], ACT.Exp).then_inc(gap_out, 1)

        @block.vector
        def _(dve):
            link = Steps(dve, step)

            def wide(x, n):
                return x.unsqueeze(2).to_broadcast([P, LT, n])

            def first_best(x, at_best, index, marks, hot, n):
                link(dve.tensor_reduce(at_best, x, AX.X, ALU.max))
                link(dve.tensor_tensor(marks, x, wide(at_best, n), ALU.is_equal))
                link(dve.scalar_tensor_tensor(marks, marks, -64.0, k.const(index).unsqueeze(1).to_broadcast([P, LT, n]), ALU.mult, ALU.add))
                link(dve.tensor_reduce(total[:, :], marks, AX.X, ALU.min))
                link(dve.tensor_tensor(hot, marks, wide(total[:, :], n), ALU.is_equal))

            dve.wait_ge(scored, 1)
            dve.wait_ge(loaded, 64)
            link(dve.tensor_tensor(logit[:, :, :], score[:, 0:LT * N].rearrange("p (t n) -> p t n", n=N),
                                   bias[:, :].unsqueeze(1).to_broadcast([P, LT, N]), ALU.add))
            link(dve.tensor_reduce(top[:, :], logit[:, :, 0:G], AX.X, ALU.max))
            dve.tensor_tensor(prob[:, :, :], logit[:, :, 0:G], wide(top[:, :], G), ALU.subtract).then_inc(exp_in, 1)
            dve.wait_ge(exp_out, 1)
            link(dve.tensor_reduce(total[:, :], prob[:, :, :], AX.X, ALU.add))
            link(dve.reciprocal(total[:, :], total[:, :]))
            link(dve.tensor_tensor(prob[:, :, :], prob[:, :, :], wide(total[:, :], G), ALU.mult))
            first_best(prob[:, :, :], gate_g[:, :], "idx4", mark4[:, :, :], group[:, :, :], G)
            link(dve.tensor_scalar(group_off[:, :, :], group[:, :, :], -1.0, -NEG, ALU.add, ALU.mult))
            for t in range(LT):
                link(dve.tensor_tensor(fine[:, t, :].rearrange("p (g e) -> p g e", e=HM_PER),
                                       logit[:, t, G:N].rearrange("p (g e) -> p g e", e=HM_PER),
                                       group_off[:, t, :].unsqueeze(2).to_broadcast([P, G, HM_PER]), ALU.add))
            first_best(fine[:, :, :], value[:, 0, :], "idx32", mark[:, :, :], best[:, 0], E)
            link(dve.scalar_tensor_tensor(fine[:, :, :], best[:, 0], 2 * NEG, fine[:, :, :], ALU.mult, ALU.add))
            first_best(fine[:, :, :], value[:, 1, :], "idx32", mark[:, :, :], best[:, 1], E)
            dve.tensor_tensor(share[:, 1, :], value[:, 1, :], value[:, 0, :], ALU.subtract).then_inc(gap_in, 1)
            dve.wait_ge(gap_out, 1)
            link(dve.tensor_scalar(total[:, :], share[:, 1, :], 1.0, None, ALU.add))
            link(dve.reciprocal(total[:, :], total[:, :]))
            link(dve.tensor_tensor(share[:, 0, :], total[:, :], gate_g[:, :], ALU.mult))
            link(dve.tensor_tensor(share[:, 1, :], share[:, 1, :], share[:, 0, :], ALU.mult))
            link(dve.tensor_tensor(gate[:, :, :], best[:, 0], wide(share[:, 0, :], E), ALU.mult))
            link(dve.tensor_tensor(mark[:, :, :], best[:, 1], wide(share[:, 1, :], E), ALU.mult))
            link(dve.tensor_tensor(gate[:, :, :], gate[:, :, :], mark[:, :, :], ALU.add))
            dve.tensor_tensor(chosen[:, :, :], best[:, 0], best[:, 1], ALU.add).then_inc(chosen_ready, 1)
            dve.wait_ge(counted, 1)
            dve.wait_ge(chosen_ready, 1)
            link(dve.tensor_tensor(rank[:, :, :].rearrange("p t e -> p (t e)"), count[:, 0:LT * E],
                                   chosen[:, :, :].rearrange("p t e -> p (t e)"), ALU.mult))
            link(dve.tensor_reduce(most[:, :], count[:, LT * E:(LT + 1) * E], AX.X, ALU.max))
            n = L // SLOTS
            link(dve.tensor_scalar(over[:, :], k.const("slots")[:, 0:n], float(SLOTS), -float(SLOTS), ALU.mult, ALU.add))
            link(dve.tensor_tensor(over[:, :], most[:, :].to_broadcast([P, n]), over[:, :], ALU.is_gt))
            link(dve.tensor_reduce(most[:, :], over[:, :], AX.X, ALU.add))
            link(dve.tensor_copy(rounds[:, :], most[:, :]))


def next_round(k, rank):
    ctx, sb, ps, sem = stage(k, "hm_next")
    with ctx:
        done = sem("done")
        block = ctx.enter_context(k.nc.Block())

        @block.vector
        def _(dve):
            dve.tensor_scalar(rank[:, :, :], rank[:, :, :], -float(SLOTS), None, ALU.add).then_inc(done, 1)
            dve.wait_ge(done, 1)


def final_norm(k, x, y_out):
    nc = k.nc
    ctx, sb, ps, sem = stage(k, "final")
    with ctx:
        square, gain, y = sb("square", [P, D]), sb("gain", [P, D]), sb("y", [P, LT, D])
        ss, rstd = sb("ss", [P, LT]), sb("rstd", [P, LT])
        loaded, stored, root_ready, row_ready, act_step, step = (sem(x) for x in ("loaded", "stored", "root_ready", "row_ready", "act_step", "step"))
        block = ctx.enter_context(nc.Block())
        out_rows = rows_view(y_out)

        @block.sync
        def _(sp):
            sp.dma_start(gain[:, :], k.dram["final_norm_g_2"].unsqueeze(0).to_broadcast([P, D])).then_inc(loaded, 16)
            for t in range(LT):
                sp.wait_ge(row_ready, t + 1)
                sp.dma_start(out_rows[:, t, :], y[:, t, :]).then_inc(stored, 16)
            sp.wait_ge(stored, 16 * LT)

        @block.scalar
        def _(act):
            link = Steps(act, act_step)
            for t in range(LT):
                link(act.activation(square[:, :], x[:, t, :], ACT.Square, accum_out=ss[:, t:t + 1]))
            act.activation(rstd[:, :], ss[:, :], ACT.Sqrt, scale=1.0 / D, bias=k.const("eps")).then_inc(root_ready, 1)

        @block.vector
        def _(dve):
            link = Steps(dve, step)
            dve.wait_ge(root_ready, 1)
            dve.wait_ge(loaded, 16)
            link(dve.reciprocal(rstd[:, :], rstd[:, :]))
            for t in range(LT):
                dve.scalar_tensor_tensor(y[:, t, :], x[:, t, :], rstd[:, t:t + 1], gain[:, :], ALU.mult, ALU.mult).then_inc(row_ready, 1)


def second_experts(k, x_in, y_out, dump=None):
    nc = k.nc
    vec2 = k.second
    dump = dump or (lambda name, ap: None)

    def tile(scope, name, shape, dt=F32):
        return scope.enter_context(nc.sbuf_tensor(name, shape, dt))

    with ExitStack() as outer:
        out = tile(outer, "hm_out", [P, LT, D])
        load(k, "hm_load", [(out[:, :, :], rows_view(x_in))])
        with ExitStack() as s:
            xn = tile(s, "hm_xn", [P, LT, D])
            rank, gate, rounds = tile(s, "hm_rank", [P, LT, HM_E]), tile(s, "hm_gate", [P, LT, HM_E]), tile(s, "hm_rounds", [P, 1], I32)
            scale = vec2[:, W2_FFN:W2_FFN + KD]
            with ExitStack() as s1:
                load_constants(k, s1, "moe")
                h3T = tile(s1, "hm_h3T", [P, KD, L])
                norm_transpose(k, "hm_norm", out, LT, h3T, scale, xn=xn)
                choose_experts(k, h3T, rank, gate, rounds)
            dump("hm_rank", rank)
            dump("hm_gate", gate)

            def gate_up(e, s, dst):
                return [(dst.rearrange("p k a n -> p k (a n)"), expert_weights(k.dram["moe_w_gu_2"], e).rearrange("(k p) n -> p k n", p=P))]

            n_rounds = nc.values_load(rounds[0:1, 0:1], min_val=1, max_val=L // SLOTS)
            with nc.Fori(0, n_rounds):
                run_experts(k, "hm", HM_E, HM_FF, gate_up, lambda e, s: expert_weights(k.dram["moe_w_down_2"], e), xn, rank, gate, scale, None, out)
                next_round(k, rank)
        final_norm(k, out, y_out)


def two_blocks(nc, dram, out):
    k = Kernel(nc, dram)
    between = [nc.dram_tensor(f"between_{i}", [1, L, D], F32, kind="Internal").ap() for i in range(3)]

    def tile(scope, name, shape):
        return scope.enter_context(nc.sbuf_tensor(name, shape, F32))

    with ExitStack() as everything:
        load_constants(k, everything, "all")
        with ExitStack() as first:
            k.first = tuple(tile(first, n, s) for n, s in (("vec", [P, 120]), ("taps", [P, 120]), ("mod", [P, 48, 2]),
                                                           ("scales", [P, 3 * KD]), ("gains", [P, 2, KD]), ("gnorm", [P, 16])))
            first_mixer(k, dram["x"], between[0])
            first_experts(k, between[0], between[1])
        k.second = tile(everything, "vec_second", [P, 40])
        second_mixer(k, between[1], between[2])
        second_experts(k, between[2], out)


def kernel(**inputs):
    import concourse.bacc as bacc
    from concourse.bass_utils import run_bass_kernel_spmd as run

    nc = bacc.Bacc("TRN2", target_bir_lowering=False, num_devices=1)
    laid_out = {n: np.ascontiguousarray(a) for n, a in inputs.items()}
    laid_out["rpb_padded"] = np.pad(np.asarray(inputs["na_rpb"]).reshape(-1), RPB_PAD)
    laid_out["constants"] = np.concatenate(list(constant_blocks().values()), 1)
    dram = {n: nc.dram_tensor(f"in_{n}", a.shape, mybir.dt.from_np(a.dtype), kind="ExternalInput").ap() for n, a in laid_out.items()}
    out = nc.dram_tensor("out", [1, L, D], F32, kind="ExternalOutput").ap()
    two_blocks(nc, dram, out)
    result = run(nc, [{f"in_{n}": a for n, a in laid_out.items()}], core_ids=[0])
    return result.results[0]["out"]
```
